# Optimizing a Trainium2 kernel written in Bass

```python
import math
import jax, jax.numpy as jnp
from jax import lax
import numpy as np

D_MODEL = 1024
BATCH = 1
SEQ = 128
DEPTH = 2
DEC_BATCH = 1
DEC_SEQ = 256
PAST_LEN = 128

GRID_W = 64
N_MIXERS = 2
N_ATTN_LAYERS = (DEPTH + 1) // 2
N_HYENA_LAYERS = DEPTH // 2
N_HEADS = 16
N_KV_HEADS = 4
HEAD_DIM = 64
ROPE_THETA = 10000.0
Q_BLOCK = 128
HYENA_ORDER = 2
SHORT_CONV = 3
FILTER_BANDS = 8
FILTER_FEAT = 1 + 2 * FILTER_BANDS
FILTER_HIDDEN = 64
N_GROUPS = 4
EXPERTS_PER_GROUP = 8
N_EXPERTS = N_GROUPS * EXPERTS_PER_GROUP
TOP_K_IN_GROUP = 2
EXPERT_HIDDEN = D_MODEL // 4
EPS = 1e-6

kernel_name = "hybrid_attn_hyena_hmoe_diffusion_step"

def rmsnorm(x, gain):
    xf = x.astype(jnp.float32)
    y = xf * lax.rsqrt(jnp.mean(xf * xf, axis=-1, keepdims=True) + EPS)
    return (y * gain.astype(jnp.float32)).astype(x.dtype)

def adaln(cond, w, b):
    ada = jax.nn.silu(cond) @ w + b
    ada = ada.reshape(cond.shape[0], 6, D_MODEL)[:, :, None, :]
    return [ada[:, i] for i in range(6)]

def modulate(h, shift, scale):
    return h * (1.0 + scale) + shift

def axial_rope_tables(L):
    rows = L // GRID_W
    row = jnp.repeat(jnp.arange(rows, dtype=jnp.float32), GRID_W)
    col = jnp.tile(jnp.arange(GRID_W, dtype=jnp.float32), rows)
    axis_dim = HEAD_DIM // 2
    inv_freq = ROPE_THETA ** (-jnp.arange(0, axis_dim, 2, dtype=jnp.float32) / axis_dim)
    ang_r = row[:, None] * inv_freq[None, :]
    ang_c = col[:, None] * inv_freq[None, :]
    return (jnp.cos(ang_r), jnp.sin(ang_r), jnp.cos(ang_c), jnp.sin(ang_c))

def rotate_axis(x, cos, sin):
    x1, x2 = jnp.split(x, 2, axis=-1)
    return jnp.concatenate([x1 * cos - x2 * sin, x2 * cos + x1 * sin], axis=-1)

def apply_axial_rope(x, tables):
    cos_r, sin_r, cos_c, sin_c = tables
    xf = x.astype(jnp.float32)
    xr, xc = jnp.split(xf, 2, axis=-1)
    out = jnp.concatenate([rotate_axis(xr, cos_r, sin_r), rotate_axis(xc, cos_c, sin_c)], axis=-1)
    return out.astype(x.dtype)

def block_attention(q, k, v):
    B, Hq, Lq, Dh = q.shape
    G = Hq // N_KV_HEADS
    nb = Lq // Q_BLOCK
    qb = jnp.moveaxis(q.reshape(B, N_KV_HEADS, G, nb, Q_BLOCK, Dh), 3, 0)
    scale = Dh ** -0.5

    def one_block(qblk):
        s = jnp.einsum('bkgqd,bksd->bkgqs', qblk, k, preferred_element_type=jnp.float32) * scale
        p = jax.nn.softmax(s, axis=-1)
        return jnp.einsum('bkgqs,bksd->bkgqd', p.astype(v.dtype), v)

    out = lax.map(one_block, qb)
    return jnp.moveaxis(out, 0, 3).reshape(B, Hq, Lq, Dh)

def attn_qkv(h, w_q, w_kv, q_gain, k_gain):
    B, L, _ = h.shape
    q = (h @ w_q).reshape(B, L, N_HEADS, HEAD_DIM)
    kv = (h @ w_kv).reshape(B, L, 2, N_KV_HEADS, HEAD_DIM)
    k, v = kv[:, :, 0], kv[:, :, 1]
    q = rmsnorm(q, q_gain)
    k = rmsnorm(k, k_gain)
    return q.transpose(0, 2, 1, 3), k.transpose(0, 2, 1, 3), v.transpose(0, 2, 1, 3)

def attn_out(o, w_o):
    B, H, L, Dh = o.shape
    return o.transpose(0, 2, 1, 3).reshape(B, L, H * Dh) @ w_o

def short_conv(u, w, b):
    L = u.shape[1]
    pad = SHORT_CONV // 2
    up = jnp.pad(u, ((0, 0), (pad, pad), (0, 0)))
    return sum(up[:, i:i + L] * w[i] for i in range(SHORT_CONV)) + b

def implicit_filters(L, w1, b1, w2, b2, w3, b3, freq, log_decay):
    f32 = jnp.float32
    t_norm = jnp.linspace(0.0, 1.0, L, dtype=f32)[:, None]
    bands = jnp.linspace(1e-4, FILTER_BANDS - 1, FILTER_BANDS, dtype=f32)[None, :]
    w = (2.0 * math.pi) * jnp.arange(L, dtype=f32)[:, None] / L
    feats = jnp.concatenate([t_norm, jnp.cos(bands * w), -jnp.sin(bands * w)], axis=-1)
    fr = freq.astype(f32)
    hdn = jnp.sin(fr * (feats @ w1.astype(f32) + b1.astype(f32)))
    hdn = jnp.sin(fr * (hdn @ w2.astype(f32) + b2.astype(f32)))
    filt = hdn @ w3.astype(f32) + b3.astype(f32)
    filt = filt * jnp.exp(-t_norm * jnp.exp(log_decay.astype(f32))[None, :])
    filt = filt.reshape(L, HYENA_ORDER, 2, D_MODEL).transpose(1, 2, 0, 3)
    norm = jnp.sum(jnp.abs(filt), axis=(1, 2), keepdims=True)
    return filt / (norm + EPS)

def bidirectional_long_conv(z, h_fwd, h_bwd):
    L = z.shape[1]
    first = h_fwd.at[0].add(h_bwd[0])
    circ = jnp.concatenate([first, jnp.zeros((1, D_MODEL), jnp.float32), jnp.flip(h_bwd[1:], axis=0)], axis=0)
    zf = jnp.fft.rfft(z.astype(jnp.float32), n=2 * L, axis=1)
    cf = jnp.fft.rfft(circ, n=2 * L, axis=0)
    y = jnp.fft.irfft(zf * cf[None], n=2 * L, axis=1)[:, :L]
    return y.astype(z.dtype)

def hyena_mixer(h, w_in, b_in, sw, sb, fw1, fb1, fw2, fb2, fw3, fb3, ffreq, log_decay, skip, w_out, b_out):
    L = h.shape[1]
    u = short_conv(h @ w_in + b_in, sw, sb)
    x1, x2, v = jnp.split(u, 3, axis=-1)
    filt = implicit_filters(L, fw1, fb1, fw2, fb2, fw3, fb3, ffreq, log_decay)
    z = v
    for o, gate in enumerate((x1, x2)):
        z = gate * (bidirectional_long_conv(z, filt[o, 0], filt[o, 1]) + skip[o] * z)
    return z @ w_out + b_out

def hierarchical_moe(h, wg, bg, we, be, w_gate, w_up, w_down):
    B, L, D = h.shape
    t = h.reshape(B * L, D)
    g_logits = (t @ wg + bg).astype(jnp.float32)
    g_prob = jax.nn.softmax(g_logits, axis=-1)
    g_idx = jnp.argmax(g_logits, axis=-1)
    g_top = jnp.max(g_prob, axis=-1, keepdims=True)
    e_logits = (jnp.einsum('nd,dge->nge', t, we) + be).astype(jnp.float32)
    e_in_group = jnp.einsum('nge,ng->ne', e_logits, jax.nn.one_hot(g_idx, N_GROUPS, dtype=jnp.float32))
    e_val, e_idx = lax.top_k(e_in_group, TOP_K_IN_GROUP)
    e_w = jax.nn.softmax(e_val, axis=-1) * g_top
    expert_id = g_idx[:, None] * EXPERTS_PER_GROUP + e_idx
    combine = jnp.sum(jax.nn.one_hot(expert_id, N_EXPERTS, dtype=jnp.float32) * e_w[..., None], axis=1)
    a = jnp.einsum('nd,edh->neh', t, w_gate)
    b = jnp.einsum('nd,edh->neh', t, w_up)
    act = jax.nn.silu(a) * b * combine[:, :, None].astype(t.dtype)
    out = jnp.einsum('neh,ehd->nd', act, w_down)
    return out.reshape(B, L, D)

def _trunk(x, cond, p, cache_k, cache_v):
    latent = cache_k is not None
    rope = axial_rope_tables(x.shape[1]) if latent else None
    ctx_k, ctx_v = [], []
    for l in range(DEPTH):
        sh1, sc1, g1, sh2, sc2, g2 = adaln(cond, p['w_ada'][l], p['b_ada'][l])
        h = modulate(rmsnorm(x, p['norm_mix'][l]), sh1, sc1)
        if l % N_MIXERS == 0:
            a = l // N_MIXERS
            q, k, v = attn_qkv(h, p['attn_w_q'][a], p['attn_w_kv'][a], p['attn_q_norm'][a], p['attn_k_norm'][a])
            if latent:
                q = apply_axial_rope(q, rope)
                k = apply_axial_rope(k, rope)
                k_all = jnp.concatenate([k, cache_k[:, a].astype(k.dtype)], axis=2)
                v_all = jnp.concatenate([v, cache_v[:, a].astype(v.dtype)], axis=2)
            else:
                ctx_k.append(k)
                ctx_v.append(v)
                k_all, v_all = k, v
            mix = attn_out(block_attention(q, k_all, v_all), p['attn_w_o'][a])
        else:
            j = l // N_MIXERS
            mix = hyena_mixer(h, p['hy_w_in'][j], p['hy_b_in'][j], p['hy_short_w'][j], p['hy_short_b'][j],
                              p['hy_filt_w1'][j], p['hy_filt_b1'][j], p['hy_filt_w2'][j], p['hy_filt_b2'][j],
                              p['hy_filt_w3'][j], p['hy_filt_b3'][j], p['hy_filt_freq'][j], p['hy_log_decay'][j],
                              p['hy_skip'][j], p['hy_w_out'][j], p['hy_b_out'][j])
        x = x + g1 * mix
        h = modulate(rmsnorm(x, p['norm_ffn'][l]), sh2, sc2)
        x = x + g2 * hierarchical_moe(h, p['router_group_w'][l], p['router_group_b'][l],
                                      p['router_expert_w'][l], p['router_expert_b'][l],
                                      p['moe_w_gate'][l], p['moe_w_up'][l], p['moe_w_down'][l])
    y = rmsnorm(x, p['final_norm'])
    if latent:
        return y, None, None
    return y, jnp.stack(ctx_k, axis=1), jnp.stack(ctx_v, axis=1)

def setup_inputs(seed: int = 0) -> dict:
    key = jax.random.key(seed)
    ks = jax.random.split(key, 40)
    f32 = jnp.float32

    def nrm(k, shape, scale):
        return jax.random.normal(k, shape, f32) * scale

    D = D_MODEL
    NA, NH = N_ATTN_LAYERS, N_HYENA_LAYERS
    kv_shape_dec = (DEC_BATCH, NA, N_KV_HEADS, PAST_LEN, HEAD_DIM)
    return {
        'x_prompt': nrm(ks[0], (BATCH, SEQ, D), 1.0),
        'x_sample': nrm(ks[1], (DEC_BATCH, DEC_SEQ, D), 1.0),
        'cache_k': nrm(ks[2], kv_shape_dec, 1.0),
        'cache_v': nrm(ks[3], kv_shape_dec, 1.0),
        'c': nrm(ks[4], (DEC_BATCH, D), 1.0),
        'c_ctx': nrm(ks[5], (D,), 1.0),
        'w_ada': nrm(ks[6], (DEPTH, D, 6 * D), D ** -0.5),
        'b_ada': nrm(ks[7], (DEPTH, 6 * D), 0.02),
        'norm_mix': 1.0 + nrm(ks[8], (DEPTH, D), 0.1),
        'norm_ffn': 1.0 + nrm(ks[9], (DEPTH, D), 0.1),
        'attn_w_q': nrm(ks[10], (NA, D, N_HEADS * HEAD_DIM), D ** -0.5),
        'attn_w_kv': nrm(ks[11], (NA, D, 2 * N_KV_HEADS * HEAD_DIM), D ** -0.5),
        'attn_q_norm': 1.0 + nrm(ks[12], (NA, HEAD_DIM), 0.1),
        'attn_k_norm': 1.0 + nrm(ks[13], (NA, HEAD_DIM), 0.1),
        'attn_w_o': nrm(ks[14], (NA, N_HEADS * HEAD_DIM, D), (N_HEADS * HEAD_DIM) ** -0.5),
        'hy_w_in': nrm(ks[15], (NH, D, 3 * D), D ** -0.5),
        'hy_b_in': nrm(ks[16], (NH, 3 * D), 0.02),
        'hy_short_w': nrm(ks[17], (NH, SHORT_CONV, 3 * D), SHORT_CONV ** -0.5),
        'hy_short_b': nrm(ks[18], (NH, 3 * D), 0.02),
        'hy_filt_w1': nrm(ks[19], (NH, FILTER_FEAT, FILTER_HIDDEN), FILTER_FEAT ** -0.5),
        'hy_filt_b1': nrm(ks[20], (NH, FILTER_HIDDEN), 0.1),
        'hy_filt_w2': nrm(ks[21], (NH, FILTER_HIDDEN, FILTER_HIDDEN), FILTER_HIDDEN ** -0.5),
        'hy_filt_b2': nrm(ks[22], (NH, FILTER_HIDDEN), 0.1),
        'hy_filt_w3': nrm(ks[23], (NH, FILTER_HIDDEN, 2 * HYENA_ORDER * D), FILTER_HIDDEN ** -0.5),
        'hy_filt_b3': nrm(ks[24], (NH, 2 * HYENA_ORDER * D), 0.1),
        'hy_filt_freq': 1.0 + nrm(ks[25], (NH, FILTER_HIDDEN), 0.1),
        'hy_log_decay': jax.random.uniform(ks[26], (NH, 2 * HYENA_ORDER * D), f32, math.log(3.0), math.log(15.0)),
        'hy_skip': nrm(ks[27], (NH, HYENA_ORDER, D), 0.1),
        'hy_w_out': nrm(ks[28], (NH, D, D), D ** -0.5),
        'hy_b_out': nrm(ks[29], (NH, D), 0.02),
        'router_group_w': nrm(ks[30], (DEPTH, D, N_GROUPS), D ** -0.5),
        'router_group_b': nrm(ks[31], (DEPTH, N_GROUPS), 0.01),
        'router_expert_w': nrm(ks[32], (DEPTH, D, N_GROUPS, EXPERTS_PER_GROUP), D ** -0.5),
        'router_expert_b': nrm(ks[33], (DEPTH, N_GROUPS, EXPERTS_PER_GROUP), 0.01),
        'moe_w_gate': nrm(ks[34], (DEPTH, N_EXPERTS, D, EXPERT_HIDDEN), D ** -0.5),
        'moe_w_up': nrm(ks[35], (DEPTH, N_EXPERTS, D, EXPERT_HIDDEN), D ** -0.5),
        'moe_w_down': nrm(ks[36], (DEPTH, N_EXPERTS, EXPERT_HIDDEN, D), EXPERT_HIDDEN ** -0.5),
        'final_norm': 1.0 + nrm(ks[37], (D,), 0.1),
    }

def reference(x_prompt, x_sample, cache_k, cache_v, c, c_ctx, w_ada, b_ada, norm_mix, norm_ffn,
              attn_w_q, attn_w_kv, attn_q_norm, attn_k_norm, attn_w_o,
              hy_w_in, hy_b_in, hy_short_w, hy_short_b, hy_filt_w1, hy_filt_b1, hy_filt_w2, hy_filt_b2,
              hy_filt_w3, hy_filt_b3, hy_filt_freq, hy_log_decay, hy_skip, hy_w_out, hy_b_out,
              router_group_w, router_group_b, router_expert_w, router_expert_b,
              moe_w_gate, moe_w_up, moe_w_down, final_norm):
    p = dict(w_ada=w_ada, b_ada=b_ada, norm_mix=norm_mix, norm_ffn=norm_ffn,
             attn_w_q=attn_w_q, attn_w_kv=attn_w_kv, attn_q_norm=attn_q_norm, attn_k_norm=attn_k_norm,
             attn_w_o=attn_w_o, hy_w_in=hy_w_in, hy_b_in=hy_b_in, hy_short_w=hy_short_w, hy_short_b=hy_short_b,
             hy_filt_w1=hy_filt_w1, hy_filt_b1=hy_filt_b1, hy_filt_w2=hy_filt_w2, hy_filt_b2=hy_filt_b2,
             hy_filt_w3=hy_filt_w3, hy_filt_b3=hy_filt_b3, hy_filt_freq=hy_filt_freq, hy_log_decay=hy_log_decay,
             hy_skip=hy_skip, hy_w_out=hy_w_out, hy_b_out=hy_b_out,
             router_group_w=router_group_w, router_group_b=router_group_b,
             router_expert_w=router_expert_w, router_expert_b=router_expert_b,
             moe_w_gate=moe_w_gate, moe_w_up=moe_w_up, moe_w_down=moe_w_down, final_norm=final_norm)
    cond_ctx = jnp.broadcast_to(c_ctx[None, :], (x_prompt.shape[0], D_MODEL))
    y_prompt, new_k, new_v = _trunk(x_prompt, cond_ctx, p, None, None)
    y_sample, _, _ = _trunk(x_sample, c, p, cache_k, cache_v)
    return (y_prompt, y_sample, new_k, new_v)


_drawn_inputs = setup_inputs


def setup_inputs(seed=0):
    import zlib

    import numpy as np

    out = dict(_drawn_inputs(seed))
    spreads = {}
    factors = {'hy_b_in': 4.019, 'hy_short_b': 3.219, 'router_group_b': 2.819}
    for name, (base, spread) in spreads.items():
        noise = np.random.default_rng([zlib.crc32(name.encode()), seed]).standard_normal(out[name].shape)
        drawn = base * np.exp(spread * noise) if base else spread * noise
        out[name] = __import__('jax').numpy.asarray(drawn.astype(out[name].dtype))
    for name, factor in factors.items():
        out[name] = (out[name] * factor).astype(out[name].dtype)
    return out
```

```python
import numpy as np
import concourse.bass as bass
from concourse import mybir
from contextlib import ExitStack

F32 = mybir.dt.float32
I32 = mybir.dt.int32
U32 = mybir.dt.uint32
ALU = mybir.AluOpType
ACT = mybir.ActivationFunctionType
AX = mybir.AxisListType

P = 128
D = 1024
KD = D // P
SEQ, DEC = 128, 256
T = SEQ + DEC
TC = T // P
GRID_W = 64
DEPTH = 2
HD = 64
NH, NKV = 16, 4
NG, EG = 4, 8
NE = NG * EG
EH = D // 4
PAIRS = NE // 2
WIN = 64
NWIN = T // WIN
BANDS = 8
FEAT = 1 + 2 * BANDS
FH = 64
EPS = 1e-6
NONE = 100000
HALF = 512
NORM_CH = 2
SPANS = ((0, SEQ), (SEQ, T))

R_BADA, R_NMIX, R_NFFN, R_FIN, R_BIN = 0, 96, 112, 128, 136
R_SW, R_SB, R_SKIP, R_BOUT, R_C, R_CCTX, R_QN, R_KN = 160, 232, 256, 272, 280, 288, 296, 297
R_END = 298

PER_LAYER = dict(
    logit_mm=1, htok_mm=6, htok_set0_=3, htok_set1_=3, mask_set=1, place_mm=1, cum_set=1, tab_in=16, lg_set=1,
    gather0_=8 * PAIRS, gather1_=8 * PAIRS, turn_mm=PAIRS + 1, dn_mm=PAIRS + 1, gu_mm=PAIRS, act_set=PAIRS + 1,
    at_mm=PAIRS, at_set=PAIRS, y_set=2 * PAIRS + 2, gt_set=2 * PAIRS, silu=PAIRS,
    y_free=PAIRS + 2, ysum=1, res_mm=KD, moe_add=2 * KD, gsub_set=1, gexp=2, dv_set=1, slots_set=1,
    h_rows=16 * TC, tab_fill=32 * TC, slots=PAIRS, scatter=16 * PAIRS, rows_done=1, y2_in=32, g_clear=2,
    gu_in=16 * PAIRS, dn_in=8 * PAIRS)


def constants():
    cols = {}
    p = np.arange(P)
    cols["ident"] = np.eye(P)
    cols["ones"] = np.ones((P, P))
    cols["headones"] = (p[:, None] // HD == p[None, :] // HD) * 1.0
    rot = np.zeros((P, P))
    for d in range(P):
        if d % 32 < 16:
            rot[d + 16, d] = -1.0
        else:
            rot[d - 16, d] = 1.0
    cols["rot"] = rot
    t = np.arange(DEC)
    d = p % HD
    ax = HD // 2
    inv = (10000.0 ** (-np.arange(0, ax, 2, dtype=np.float32) / ax)).astype(np.float32)
    pos = np.where(d[:, None] < ax, (t // GRID_W)[None, :], (t % GRID_W)[None, :]).astype(np.float32)
    ang = pos * inv[d % 16][:, None]
    cols["cos"], cols["sin"] = np.cos(ang), np.sin(ang)
    for L in (SEQ, DEC):
        n = 2 * L
        tt, f = np.arange(L), np.arange(L)
        w = 2 * np.pi * ((tt[:, None] * f[None, :]) % n) / n
        alt = (-1.0) ** tt
        re, im = np.cos(w), -np.sin(w)
        im0 = im.copy()
        im0[:, 0] = 0.0
        imz = im0.copy()
        imz[:, 0] = alt
        fold = lambda m: m.reshape(L // P, P, -1).transpose(1, 0, 2).reshape(P, -1)
        cols[f"fwd{L}"] = fold(np.concatenate([re, imz], 1))
        cols[f"alt{L}"] = fold(2 * alt[:, None])
        wt = np.where(f == 0, 1.0, 2.0)[:, None] / n
        inv_re, inv_im = wt * re.T, wt * im0.T
        inv_im[0] = alt / n
        both = np.concatenate([inv_re, inv_im], 0)
        cols[f"inv{L}"] = both.reshape(2 * L // P, P, L).transpose(1, 0, 2).reshape(P, -1)
    feats, tneg = [], []
    for L in (SEQ, DEC):
        tn = np.linspace(0.0, 1.0, L, dtype=np.float32)
        bands = np.linspace(1e-4, BANDS - 1, BANDS, dtype=np.float32)[None, :]
        w = np.float32(2.0 * np.pi) * np.arange(L, dtype=np.float32)[:, None] / np.float32(L)
        a = (bands * w).astype(np.float64)
        feats.append(np.concatenate([tn[:, None], np.cos(a), -np.sin(a)], 1).T)
        tneg.append(-tn.reshape(-1, P).T)
    ft = np.zeros((P, T))
    ft[:FEAT] = np.concatenate(feats, 1)
    cols["feats"] = ft
    cols["tneg"] = np.concatenate(tneg, 1)
    cols["before"] = (p[:, None] < p[None, :]) * 1.0
    cols["prio"] = np.tile(np.concatenate([np.arange(NG, 0, -1), np.arange(EG, 0, -1)]), (P, 1)) * 1.0
    e = np.arange(NE)
    cols["rowbase"] = np.tile((e % 2) * (WIN * PAIRS) + e // 2, (P, 1)) * 1.0
    last = ("cos", "sin", "feats")
    at, parts, where = 0, [], {}
    for name in [n for n in cols if n not in last] + list(last):
        where[name] = (at, at + cols[name].shape[1])
        at += cols[name].shape[1]
        parts.append(np.asarray(cols[name], np.float32))
    return np.concatenate(parts, 1), where


CONST, WHERE = constants()
KEPT = WHERE["cos"][0]


def token_rows():
    a = np.zeros((P, TC, 2, 4), np.int32)
    tok = np.arange(P)[:, None] + P * np.arange(TC)[None, :]
    for k in range(2):
        a[:, :, k, 0] = tok
        a[:, :, k, 1] = tok + k * T
    return a.reshape(P, TC * 8)


def build(nc, a):
    ctx = ExitStack()
    with ctx:
        def sb(name, shape, dt=F32):
            return ctx.enter_context(nc.sbuf_tensor(name, shape, dt))

        sems = {}

        def sem(name):
            if name not in sems:
                sems[name] = ctx.enter_context(nc.semaphore(name))
            return sems[name]

        hD = nc.dram_tensor("h_rows", [T, D], F32, kind="Internal").ap()
        yD = nc.dram_tensor("expert_rows", [2 * T, D], F32, kind="Internal").ap()
        tabD = [nc.dram_tensor(f"slot_table{l}", [NWIN * P * PAIRS, 4], I32, kind="Internal").ap()
                for l in range(DEPTH)]
        cfD = [nc.dram_tensor(f"filter_spectra{o}", [P, 6, D], F32, kind="Internal").ap() for o in range(2)]

        const = sb("const", [P, KEPT])
        C = {n: const[:, lo:hi] for n, (lo, hi) in WHERE.items() if hi <= KEPT}
        ident, ones = C["ident"], C["ones"]
        xT = sb("xT", [P, KD, T])
        hT = sb("hT", [P, KD, T])
        pc = sb("pc", [P, R_END])
        condS = sb("condS", [P, KD, 32])
        ada = sb("ada", [P, DEPTH, 6, KD, 2])
        amul = sb("amul", [P, DEPTH, 2, KD, 2])
        gbo = sb("gbo", [P, KD, 2])
        rstd = sb("rstd", [P, T])
        sq = sb("sq", [P, 2, T])
        rout = sb("rout", [P, DEPTH, KD, NG + NE])
        rbias = sb("rbias", [P, DEPTH, NG + NE])
        trow = sb("trow", [P, TC * 8], I32)
        cumx = sb("cumx", [1, PAIRS + 1], I32)
        fcol = sb("fcol", [FH, 4])
        ring = sb("ring", [P, 24576])
        WORK = 15360
        work = sb("work", [P, WORK])

        def ws(lo, n):
            assert lo + n <= WORK, (lo, n)
            return work[:, lo:lo + n]

        bank = [ctx.enter_context(nc.psum_tensor(f"bank{i}", [P, HALF], F32)) for i in range(8)]

        xtok = ws(0, TC * D).rearrange("p (c d) -> p c d", c=TC)
        prow = ws(3072, 3 * P).rearrange("p (c d) -> p c d", c=3)
        none_tile = ws(3456, NWIN * PAIRS * 4).bitcast(I32)
        w3a = ws(0, 4096)
        eld = ws(4096, 2048).rearrange("p (b d c) -> p b d c", b=2, d=2)
        hfb = ws(6144, 3072).rearrange("p (d t c) -> p d t c", d=2, t=3)
        dec = ws(9216, 1024).rearrange("p (b c) -> p b c", b=2)
        absb = ws(10240, 1024).rearrange("p (b c) -> p b c", b=2)
        smdf = ws(11264, 3072).rearrange("p (d t c) -> p d t c", d=2, t=3)
        rn = ws(14336, 1024).rearrange("p (b c) -> p b c", b=2)
        hd1 = sb("hd1", [P, 2, T])
        w1 = hd1[0:FEAT, 1, 0:FH]
        w2 = ws(7680, FH)[0:FH, :]
        cfb = hT[:, :, :].rearrange("p k t -> p (k t)")[:, 0:3072].rearrange("p (b c) -> p b c", b=6)
        hdr = ws(6144, 2 * T).rearrange("p (b t) -> p b t", b=2)
        hdt = ws(6144 + 2 * T, T)
        C["feats"] = ws(6144 + 3 * T, T)
        eps_col = sb("eps_col", [P, 1])
        PI_F = float(np.float32(3.1415925))
        adaR = sq[:, :, 0:256]
        qT = ws(0, 3072).rearrange("p (c t) -> p c t", c=KD)
        kT = ws(3072, 1024).rearrange("p (c t) -> p c t", c=2)
        V = ws(4096, 1024).rearrange("p (c d) -> p c d", c=4)
        oT = ws(5120, 3072).rearrange("p (c t) -> p c t", c=KD)
        prob = ws(8192, 2 * 896).rearrange("p (b c) -> p b c", b=2)
        probT = ws(9984, 2 * 896).rearrange("p (b c) -> p b c", b=2)
        raw = ws(11776, 2 * T).rearrange("p (b c) -> p b c", b=2)
        rq = ws(12544, 2 * T).rearrange("p (b c) -> p b c", b=2)
        rs_ = ws(13312, 2 * DEC).rearrange("p (b c) -> p b c", b=2)
        ck = ws(13824, 256)
        ktok = ws(14080, 256)
        C["cos"], C["sin"] = ws(14336, DEC), ws(14336 + DEC, DEC)
        sm = ws(12032, 1024)
        tab = ws(13056, NWIN * PAIRS * 4).bitcast(I32)
        hTok = ws(0, TC * D).rearrange("p (c d) -> p c d", c=TC)
        G = ws(3072, 2 * D).rearrange("p (b d) -> p b d", b=2)
        Gx = ws(5120, D)
        GT = ws(6144, D).rearrange("p (k s) -> p k s", k=KD)
        GTx = ws(7168, D).rearrange("p (k s) -> p k s", k=KD)
        S = ws(8192, EH)
        A = ws(8448, EH)
        AT = ws(8704, EH).rearrange("p (k s) -> p k s", k=2)
        Y = ws(8960, 2 * D).rearrange("p (b d) -> p b d", b=2)
        Yx = ws(11008, D)
        cur = sb("cur", [P, 2, 4], I32)
        curx = sb("curx", [P, 4], I32)
        y2 = ws(0, 2 * TC * D).rearrange("p (k c d) -> p k c d", k=2, c=TC)
        UW = T + 1
        st = ws(0, 3 * KD * UW).rearrange("p (s k t) -> p s k t", s=3, k=KD)
        upad = ws(3 * KD * UW, 2 * (UW + 2)).rearrange("p (b c) -> p b c", b=2)
        cv = ws(3 * KD * UW + 2 * (UW + 2), 2 * UW).rearrange("p (b c) -> p b c", b=2)
        HX = 3 * KD * UW + 4 * UW + 4
        ztok = hT[:, :, :].rearrange("p k t -> p (k t)").rearrange("p (c d) -> p c d", c=TC)
        prod = ws(HX, 4 * HALF).rearrange("p (b c) -> p b c", b=4)
        ztmp = ws(HX + 4 * HALF, T)
        ytmp = ws(HX + 4 * HALF + T, T)
        Yf = ring[:, 0:6 * D].rearrange("p (f c) -> p f c", f=6)
        cf = ring[:, 6 * D:12 * D].rearrange("p (f c) -> p f c", f=6)
        wout = ring[:, 12 * D:20 * D].rearrange("p (k n) -> p k n", k=KD)
        yout = ws(0, TC * D).rearrange("p (c d) -> p c d", c=TC)

        def conv_cols(lo, hi):
            return (lo, hi) if hi <= SEQ else (lo + 1, hi + 1)

        def ada_tile(n):
            return ring[:, (n % 3) * 8192:(n % 3 + 1) * 8192].rearrange("p (k n) -> p k n", k=KD)

        wq = ring[:, 0:8192].rearrange("p (k n) -> p k n", k=KD)
        wkv = ring[:, 8192:12288].rearrange("p (k n) -> p k n", k=KD)
        wo = ring[:, 12288:20480].rearrange("p (c n) -> p c n", c=KD)
        win = [ring[:, 4096 * i:4096 * (i + 1)].rearrange("p (k n) -> p k n", k=KD) for i in range(6)]
        WIN_GROUP = [0, 0, 1, 2, 2, 3]
        WIN_ORDER = [4, 5, 0, 1, 2, 3]

        def slot_gu(s):
            return ring[:, s * 12288:s * 12288 + 8192].rearrange("p (u j k h) -> p u j k h", u=2, j=2, k=KD)

        def slot_dn(s):
            return ring[:, s * 12288 + 8192:(s + 1) * 12288].rearrange("p (j k n) -> p j k n", j=2, k=2)

        at = [0]

        def small(*shape):
            n = int(np.prod(shape))
            v = sm[:, at[0]:at[0] + n]
            at[0] += n
            assert at[0] <= 1024
            if len(shape) == 2:
                return v.rearrange("p (a b) -> p a b", a=shape[0])
            if len(shape) == 3:
                return v.rearrange("p (a b c) -> p a b c", a=shape[0], b=shape[1])
            return v

        lg = small(TC, NG + NE)
        gmax, gden, v1, v2, ev, den, w1r, w2r = [small(TC, 1) for _ in range(8)]
        gx, geq, goh = [small(TC, NG) for _ in range(3)]
        esel, eeq, oh1, oh2, e2 = [small(TC, EG) for _ in range(5)]
        etmp = small(TC, EG)
        m1, m2, m_all = [small(TC, NG, EG) for _ in range(3)]
        mtmp = small(TC, NE)
        posk, rowk, wck, basek = [small(TC, 2) for _ in range(4)]
        idx = sb("idx", [P, TC * 2], I32)
        pay = sb("pay", [P, TC, 2, 4], I32)
        cnt = sb("cnt", [1, 128])
        mx = sb("mx", [P, 2, 3])
        nb = sb("nb", [P, 2, 3])
        rsum = sb("rsum", [P, 2, 3])
        rinv = sb("rinv", [P, 2, 3])

        NADA = DEPTH * 6
        FILT = [(o, n) for o in range(2) for n in range(2)]
        FILT_AFTER = {2: 0, 4: 1, 6: 2, 8: 3}
        QK = 10

        def chunk_dst(m, lo, hi):
            return kT[:, m, lo:hi] if m < 2 else qT[:, m - 2, lo:hi]

        x_in = [a["x_prompt"][0], a["x_sample"][0, 0:P], a["x_sample"][0, P:2 * P]]
        y_out = [a["out_0"][0], a["out_1"][0, 0:P], a["out_1"][0, P:2 * P]]
        rows = lambda v, n: v.rearrange("(r c) -> r c", c=P)
        param_rows = [
            (R_BADA, a["b_ada"].rearrange("l (r c) -> (l r) c", c=P)),
            (R_NMIX, a["norm_mix"].rearrange("l (r c) -> (l r) c", c=P)),
            (R_NFFN, a["norm_ffn"].rearrange("l (r c) -> (l r) c", c=P)),
            (R_FIN, rows(a["final_norm"], 8)),
            (R_BIN, rows(a["hy_b_in"][0], 24)),
            (R_SW, a["hy_short_w"][0].rearrange("w (r c) -> (w r) c", c=P)),
            (R_SB, rows(a["hy_short_b"][0], 24)),
            (R_SKIP, a["hy_skip"][0].rearrange("w (r c) -> (w r) c", c=P)),
            (R_BOUT, rows(a["hy_b_out"][0], 8)),
            (R_C, rows(a["c"][0], 8)),
            (R_CCTX, rows(a["c_ctx"], 8)),
        ]

        def prow_at(r, n):
            assert r // P == (r + n - 1) // P
            return prow[r % P:r % P + n, r // P, :]

        block = ctx.enter_context(nc.Block())

        def load_ada(sp, t):
            if t >= 3:
                sp.wait_ge(sem("ada_mm"), t - 2)
            l, s = divmod(t, 6)
            sp.dma_start(ada_tile(t), a["w_ada"][l, :, s * D:(s + 1) * D].rearrange("(k p) n -> p k n", p=P))\
                .then_inc(sem(f"ada_in{t % 3}"), 16)

        def load_decay(sp, f):
            if f >= 2:
                sp.wait_ge(sem("dec_set"), 6 * (f - 1))
            o, n = FILT[f]
            for d in range(2):
                lo = (2 * o + d) * D + n * HALF
                sp.dma_start(eld[:, f % 2, d, :], a["hy_log_decay"][0, lo:lo + HALF].partition_broadcast(P))\
                    .then_inc(sem(f"decay_in{f % 2}"), 16)

        def load_pair(sp, l, s, q, behind=False):
            gu, dn = slot_gu(s), slot_dn(s)
            for u, name in enumerate(("moe_w_gate", "moe_w_up")):
                sp.dma_start(gu[:, u].rearrange("p j k h -> p j (k h)"),
                             a[name][l, bass.ds(2 * q, 2)].rearrange("j (p k) h -> p j (k h)", p=P))\
                    .then_inc(sem(f"gu_in_{s}"), 16)
            if behind:
                sp.wait_ge(sem("dn_mm"), l * PER_LAYER["dn_mm"] + q - 1 + 1)
            sp.dma_start(dn, a["moe_w_down"][l, bass.ds(2 * q, 2)].rearrange("j (k p) n -> p j k n", p=P))\
                .then_inc(sem(f"dn_in_{s}"), 16)

        def moe_loads(sp, l):
            with sp.Fori(1, PAIRS // 2) as i:
                for s in range(2):
                    sp.wait_ge(sem("gu_mm"), l * PER_LAYER["gu_mm"] + 2 * i + s - 1)
                    load_pair(sp, l, s, 2 * i + s, behind=True)
            sp.wait_ge(sem("rows_done"), l * PER_LAYER["rows_done"] + 1)
            for k in range(2):
                sp.dma_start(y2[:, k], yD[k * T:(k + 1) * T].rearrange("(c p) d -> p c d", p=P))\
                    .then_inc(sem(f"y2_in"), 16)

        def load_win(sp, n):
            c = WIN_ORDER[n]
            sp.dma_start(win[n], a["hy_w_in"][0, :, c * HALF:(c + 1) * HALF].rearrange("(k p) n -> p k n", p=P))\
                .then_inc(sem(f"win_in{WIN_GROUP[n]}"), 16)

        def apart(eng):
            eng.sem_inc(sem("passed"), 1)

        @block.sync
        def _(sp):
            for r0, src in param_rows:
                sp.dma_start(prow_at(r0, src.shape[0]), src).then_inc(sem("tables_in"), 16)
            for r0, name in ((R_QN, "attn_q_norm"), (R_KN, "attn_k_norm")):
                for b in range(2):
                    sp.dma_start(prow[r0 % P:r0 % P + 1, 2, b * HD:(b + 1) * HD], a[name])\
                        .then_inc(sem("tables_in"), 16)
            sp.dma_start(const[:, :], a["const"][:, 0:KEPT]).then_inc(sem("tables_in"), 16)
            for c in range(TC):
                sp.dma_start(xtok[:, c, :], x_in[c]).then_inc(sem("x_in"), 16)
            for t in range(3):
                load_ada(sp, t)
            sp.dma_start(w1, a["hy_filt_w1"][0]).then_inc(sem("filt_small_in"), 16)
            sp.dma_start(C["feats"], a["const"][:, WHERE["feats"][0]:WHERE["feats"][1]]).then_inc(sem("filt_small_in"), 16)
            sp.dma_start(w2[:, :], a["hy_filt_w2"][0]).then_inc(sem("filt_small_in"), 16)
            for i, name in enumerate(("hy_filt_b1", "hy_filt_b2", "hy_filt_freq")):
                sp.dma_start(fcol[:, i:i + 1], a[name][0].rearrange("(p a) -> p a", a=1))\
                    .then_inc(sem("filt_small_in"), 16)
            sp.wait_ge(sem("preset"), 3)
            for l in range(DEPTH):
                sp.dma_start(tabD[l].rearrange("(w p q) c -> p w (q c)", w=NWIN, p=P),
                             none_tile.rearrange("p (w q) -> p w q", w=NWIN)).then_inc(sem("tab_clear"), 16)
            sp.wait_ge(sem("xT_done"), KD)
            sp.wait_ge(sem("pc_done"), 1)
            sp.wait_ge(sem("tab_clear"), 16 * DEPTH)
            sp.dma_start(w3a[0:FH, :], a["hy_filt_w3"][0]).then_inc(sem("w3_in"), 16)
            sp.dma_start(w3a[FH:FH + 1, :], a["hy_filt_b3"]).then_inc(sem("w3_in"), 16)
            load_decay(sp, 0)
            sp.dma_start(trow[:, :], a["token_rows"]).then_inc(sem("rout_in"), 16)
            for l in range(DEPTH):
                sp.dma_start(rout[:, l, :, 0:NG], a["router_group_w"][l].rearrange("(k p) g -> p k g", p=P))\
                    .then_inc(sem("rout_in"), 16)
                sp.dma_start(rout[:, l, :, NG:], a["router_expert_w"][l].rearrange("(k p) g e -> p k (g e)", p=P))\
                    .then_inc(sem("rout_in"), 16)
                sp.dma_start(rbias[:, l, 0:NG], a["router_group_b"][l].partition_broadcast(P))\
                    .then_inc(sem("rout_in"), 16)
                sp.dma_start(rbias[:, l, NG:], a["router_expert_b"][l].rearrange("g e -> (g e)").partition_broadcast(P))\
                    .then_inc(sem("rout_in"), 16)
            for t in range(3, NADA):
                load_ada(sp, t)
                if t - 3 in FILT_AFTER and FILT_AFTER[t - 3] + 1 < 4:
                    load_decay(sp, FILT_AFTER[t - 3] + 1)
            sp.wait_ge(sem("ada_mm"), NADA)
            sp.dma_start(wkv, a["attn_w_kv"][0].rearrange("(k p) n -> p k n", p=P)).then_inc(sem("wkv_in"), 16)
            sp.dma_start(wq, a["attn_w_q"][0].rearrange("(k p) n -> p k n", p=P)).then_inc(sem("wq_in"), 16)
            wo_v = a["attn_w_o"][0].rearrange("(g b m d) n -> b d g m n", g=2, b=2, m=4)
            for b in range(2):
                for g in range(2):
                    sp.dma_start(wo[b * HD:(b + 1) * HD, 4 * g:4 * g + 4, :], wo_v[b, :, g]).then_inc(sem("wo_in"), 16)
            sp.wait_ge(sem("cf_out"), 16 * 24)
            sp.dma_start(ck.rearrange("p (h d) -> p h d", h=NKV), a["cache_k"][0, 0].rearrange("h s d -> s h d"))\
                .then_inc(sem("cache_in"), 16)
            sp.dma_start(V[:, 3, :].rearrange("p (h d) -> p h d", h=NKV), a["cache_v"][0, 0].rearrange("h s d -> s h d"))\
                .then_inc(sem("cache_in"), 16)
            sp.dma_start(work[:, 14336:14336 + 2 * DEC], a["const"][:, WHERE["cos"][0]:WHERE["sin"][1]])\
                .then_inc(sem("cache_in"), 16)
            sp.wait_ge(sem("v_done"), TC)
            sp.dma_start(a["out_3"][0, 0].rearrange("h s d -> s h d"), V[:, 0, :].rearrange("p (h d) -> p h d", h=NKV))\
                .then_inc(sem("kv_out"), 16)
            sp.wait_ge(sem("ktok_done"), 1)
            sp.dma_start(a["out_2"][0, 0].rearrange("h s d -> s h d"), ktok.rearrange("p (h d) -> p h d", h=NKV))\
                .then_inc(sem("kv_out"), 16)
            sp.wait_ge(sem("qk_mm"), QK)
            sp.wait_ge(sem("v_mm"), TC)
            load_pair(sp, 0, 0, 0)
            sp.wait_ge(sem("mix0_mm"), KD)
            load_pair(sp, 0, 1, 1)
            moe_loads(sp, 0)
            sp.wait_ge(sem("gu_mm"), PAIRS - 1)
            for n in (0, 1):
                load_win(sp, n)
            sp.wait_ge(sem("dn_mm"), PAIRS - 1 + 1)
            load_win(sp, 2)
            sp.wait_ge(sem("gu_mm"), PAIRS)
            for n in (3, 4):
                load_win(sp, n)
            sp.wait_ge(sem("dn_mm"), PAIRS + 1)
            load_win(sp, 5)
            sp.wait_ge(sem("hin_mm"), 24)
            sp.wait_ge(sem("cf_out"), 16 * 24)
            sp.dma_start(cf, cfD[0]).then_inc(sem("cf_in0"), 16)
            sp.dma_start(wout, a["hy_w_out"][0].rearrange("(k p) n -> p k n", p=P)).then_inc(sem("wout_in"), 16)
            sp.wait_ge(sem("cprod"), 6)
            sp.dma_start(cf, cfD[1]).then_inc(sem("cf_in1"), 16)
            sp.wait_ge(sem("cprod"), 12)
            sp.wait_ge(sem("inv_mm"), 2 * KD)
            load_pair(sp, 1, 0, 0)
            sp.wait_ge(sem("mix1_mm"), KD)
            load_pair(sp, 1, 1, 1)
            moe_loads(sp, 1)
            for c in range(TC):
                sp.wait_ge(sem("yout_done"), 2 * (c + 1))
                sp.dma_start(y_out[c], yout[:, c, :]).then_inc(sem("y_out"), 16)
            sp.wait_ge(sem("y_out"), 16 * TC)
            sp.wait_ge(sem("kv_out"), 32)

        @block.tensor
        def _(pe):
            mm = nc.tensor.matmul
            tr = nc.tensor.transpose

            pe.wait_ge(sem("tables_in"), 16 * (len(param_rows) + 5))
            for i, n in enumerate((P, P, R_END - 2 * P)):
                last = tr(bank[7][:, i * P:i * P + n], prow[0:n, i, :], ident[0:n, 0:n])
            last.then_inc(sem("pc_mm"), 1)
            pe.wait_ge(sem("x_in"), 16 * TC)
            for k in range(KD):
                if k >= 4:
                    pe.wait_ge(sem("xT_done"), k - 3)
                for c in range(TC):
                    last = tr(bank[k % 4][:, c * P:(c + 1) * P], xtok[:, c, k * P:(k + 1) * P], ident)
                last.then_inc(sem("xT_mm"), 1)

            pe.wait_ge(sem("filt_small_in"), 16 * 6)
            mm(bank[4][0:FH, 0:T], w1, C["feats"][0:FEAT, :], start=True, stop=True).then_inc(sem("mlp_mm"), 1)
            pe.wait_ge(sem("mlp_done"), 1)
            mm(bank[5][0:FH, 0:T], w2[:, :], hd1[0:FH, 0, :], start=True, stop=True).then_inc(sem("mlp_mm"), 1)

            def ada_mm(t):
                pe.wait_ge(sem(f"ada_in{t % 3}"), 16 * (t // 3 + 1))
                if t >= 2:
                    pe.wait_ge(sem("adaR_set"), t - 1)
                w = ada_tile(t)
                for k in range(KD):
                    for j in range(4):
                        last = mm(bank[t % 2][32 * j:32 * j + 32, 0:256], condS[:, k, :],
                                  w[:, k, 256 * j:256 * j + 256], start=(k == 0), stop=(k == KD - 1))
                last.then_inc(sem("ada_mm"), 1)

            def ada_tr(t):
                pe.wait_ge(sem("adaR_set"), t + 1)
                if t >= 1:
                    pe.wait_ge(sem("ada_done"), t)
                for u in range(2):
                    last = tr(bank[2][:, u * P:(u + 1) * P], adaR[:, t % 2, u * P:(u + 1) * P], ident)
                last.then_inc(sem("ada_tr"), 1)

            def filters(f):
                o, n = FILT[f]
                if f == 0:
                    pe.wait_ge(sem("mlp_done"), 2)
                    pe.wait_ge(sem("w3_in"), 32)
                if f >= 1:
                    pe.wait_ge(sem("rn_set"), 2 * f)
                    pe.wait_ge(sem("cf_set"), 6 * f)
                for i, (d, c) in enumerate((d, c) for d in range(2) for c in range(3)):
                    g = 6 * f + i
                    if g >= 2:
                        pe.wait_ge(sem("taps_done"), g - 1)
                    lo = (2 * o + d) * D + n * HALF
                    mm(bank[4 + g % 2][:, :], hd1[0:FH + 1, 1, c * P:(c + 1) * P], w3a[0:FH + 1, lo:lo + HALF],
                       start=True, stop=True).then_inc(sem("taps_mm"), 1)
                    if i >= 1:
                        size_sum(f, i - 1)
                size_sum(f, 5)
                pe.wait_ge(sem("smdf_done"), 6 * (f + 1))
                for i in range(6):
                    g = 6 * f + i
                    if g >= 2:
                        pe.wait_ge(sem("cf_set"), g - 1)
                    b = bank[4 + g % 2]
                    r = i % 2
                    if i < 2:
                        ops = [(C["fwd256"], c * 512 + r * P, 0, 1 + c) for c in range(2)]
                    elif i < 4:
                        ops = [(C["fwd256"], c * 512 + 256 + r * P, 1, 1 + c) for c in range(2)]
                    elif i == 4:
                        ops = [(C["fwd128"], 0, 0, 0)]
                    else:
                        ops = [(C["fwd128"], P, 1, 0)]
                    if i == 0:
                        pe.wait_ge(sem("taps_done"), 6 * (f + 1))
                    top = {2: [(C["alt256"][:, c:c + 1], 1 + c) for c in range(2)], 5: [(C["alt128"], 0)]}.get(i, [])
                    for j, (m, off, d, c) in enumerate(ops):
                        last = mm(b[:, :], m[:, off:off + P], smdf[:, d, c, :], start=(j == 0),
                                  stop=(j == len(ops) - 1))
                    for j, (col, c) in enumerate(top):
                        last = mm(b[0:1, :], col, hfb[:, 1, c, :], start=False, stop=True, skip_group_check=True)
                    last.then_inc(sem("cf_mm"), 1)

            def size_sum(f, i):
                d, c = divmod(i, 3)
                g = 6 * f + i
                pe.wait_ge(sem("abs_done"), g + 1)
                b = bank[6] if c == 0 else bank[7]
                last = mm(b[:, :], ones, absb[:, g % 2, :], start=(d == 0 and c <= 1), stop=(d == 1 and c != 1))
                last.then_inc(sem("size_mm"), 1)

            pe.wait_ge(sem("cond_set"), 2)
            pe.wait_ge(sem("xT_done"), KD)
            pe.wait_ge(sem("pc_done"), 1)
            for t in range(NADA):
                ada_mm(t)
                if t >= 1:
                    ada_tr(t - 1)
                if t in FILT_AFTER:
                    filters(FILT_AFTER[t])
            ada_tr(NADA - 1)

            def norm_sums(n):
                if n > 0:
                    pe.wait_ge(sem("rt_done"), n)
                for k in range(KD):
                    pe.wait_ge(sem("sq_done"), KD * n + k + 1)
                    last = mm(bank[3][:, 0:T], ones, sq[:, k % 2, :], start=(k == 0), stop=(k == KD - 1))
                    last.then_inc(sem("sq_mm"), 1)

            norm_sums(0)
            pe.wait_ge(sem("h_done"), 2 * KD)
            pe.wait_ge(sem("wkv_in"), 16)
            pe.wait_ge(sem("cf_set"), 24)

            def qk_mm(m):
                if m == 2:
                    pe.wait_ge(sem("wq_in"), 16)
                if m >= 2:
                    pe.wait_ge(sem("raw_set"), m - 1)
                for k in range(KD):
                    if m < 2:
                        last = mm(bank[m % 2][:, 0:T], wkv[:, k, m * P:(m + 1) * P], hT[:, k, :],
                                  start=(k == 0), stop=(k == KD - 1))
                    else:
                        g, mq = divmod(m - 2, 4)
                        for b in range(2):
                            h = 8 * g + 4 * b + mq
                            last = mm(bank[m % 2][b * HD:(b + 1) * HD, 0:T], wq[:, k, h * HD:(h + 1) * HD], hT[:, k, :],
                                      start=(k == 0), stop=(k == KD - 1))
                last.then_inc(sem("qk_mm"), 1)

            def qk_ss(m):
                pe.wait_ge(sem("qsq_set"), m + 1)
                if m >= 2:
                    pe.wait_ge(sem("qrt_set"), m - 1)
                mm(bank[4 + m % 2][:, 0:T], C["headones"], sq[:, m % 2, :], start=True, stop=True).then_inc(sem("qss_mm"), 1)

            def qk_rot(m):
                pe.wait_ge(sem("qn_set"), m + 1)
                if m >= 2:
                    pe.wait_ge(sem("qs_set"), m - 1)
                mm(bank[6 + m % 2][:, 0:DEC], C["rot"], chunk_dst(m, SEQ, T), start=True, stop=True).then_inc(sem("rot_mm"), 1)

            for m in range(QK + 2):
                if m < QK:
                    qk_mm(m)
                if 1 <= m <= QK:
                    qk_ss(m - 1)
                if m >= 2:
                    qk_rot(m - 2)
            pe.wait_ge(sem("raw_set"), QK)
            for c in range(TC):
                if c >= 2:
                    pe.wait_ge(sem("v_done"), c - 1)
                for k in range(KD):
                    last = mm(bank[c % 2][:, 0:256], hT[:, k, c * P:(c + 1) * P], wkv[:, k, 256:512],
                              start=(k == 0), stop=(k == KD - 1))
                last.then_inc(sem("v_mm"), 1)
            pe.wait_ge(sem("cache_in"), 48)
            pe.wait_ge(sem("qs_set"), QK)
            pe.wait_ge(sem("qrt_set"), QK)
            for c in range(2):
                last = tr(bank[6][:, c * P:(c + 1) * P], ck[:, c * P:(c + 1) * P], ident)
            last.then_inc(sem("ck_mm"), 1)
            for c in range(2):
                last = tr(bank[7][:, c * P:(c + 1) * P], kT[:, c, 0:P], ident)
            last.then_inc(sem("ktok_mm"), 1)

            def scores(n):
                c, b = divmod(n, 2)
                g = c // 4
                if n >= 2:
                    pe.wait_ge(sem("exp_done"), 3 * (n - 1))
                X, Z = bank[2 * (n % 2)], bank[2 * (n % 2) + 1]
                r = slice(b * HD, (b + 1) * HD)
                mm(X[:, 0:T], qT[r, c, P:2 * P], kT[r, g, P:512], start=True, stop=True)
                mm(Z[:, 0:T], qT[r, c, 2 * P:3 * P], kT[r, g, P:512], start=True, stop=True)
                mm(Z[:, T:512], qT[r, c, 0:P], kT[r, g, 0:P], start=True, stop=True).then_inc(sem("score_mm"), 1)

            def prob_tr(n):
                pe.wait_ge(sem("prob_done"), 3 * (n + 1))
                if n >= 1:
                    pe.wait_ge(sem("probTa_set"), n)
                    pe.wait_ge(sem("probTb_set"), n)
                pr = prob[:, n % 2, :]
                for kc in range(3):
                    for q in range(2):
                        b, off = (bank[4], kc * 256 + q * P) if kc < 2 else (bank[5], q * P)
                        tr(b[:, off:off + P], pr[:, q * T + kc * P:q * T + (kc + 1) * P], ident)
                tr(bank[5][:, 256:T], pr[:, 768:896], ident).then_inc(sem("probT_mm"), 1)

            def values(n):
                c, b = divmod(n, 2)
                g = 2 * (c // 4) + b
                pe.wait_ge(sem("probTa_set"), n + 1)
                pe.wait_ge(sem("probTb_set"), n + 1)
                if b == 0 and c >= 2:
                    pe.wait_ge(sem("oT_set"), c - 1)
                O = bank[6 + c % 2]
                pt = probT[:, n % 2, :]
                vs = lambda kc: V[:, kc, g * HD:(g + 1) * HD]
                mm(O[b * HD:(b + 1) * HD, 0:P], vs(0), pt[:, 768:896], start=True, stop=True)
                for kc in range(3):
                    last = mm(O[b * HD:(b + 1) * HD, P:T], vs(1 + kc), pt[:, kc * 256:(kc + 1) * 256],
                              start=(kc == 0), stop=(kc == 2))
                last.then_inc(sem("oT_mm"), 1)

            pe.wait_ge(sem("v_done"), TC)
            pe.wait_ge(sem("ck_set"), 1)
            pe.wait_ge(sem("qk_done"), QK)
            pe.wait_ge(sem("ktok_done"), 1)
            for n in range(NH + 2):
                if n < NH:
                    scores(n)
                if n >= 2:
                    values(n - 2)
                if 1 <= n <= NH:
                    prob_tr(n - 1)
            pe.wait_ge(sem("wo_in"), 64)
            pe.wait_ge(sem("oT_set"), KD)
            for m in range(KD):
                if m >= 2:
                    pe.wait_ge(sem("mix0_done"), 2 * (m - 1))
                for k in range(KD):
                    last = mm(bank[m % 2][:, 0:T], wo[:, k, m * P:(m + 1) * P], oT[:, k, :],
                              start=(k == 0), stop=(k == KD - 1))
                last.then_inc(sem("mix0_mm"), 1)

            def mm_mask(c):
                return m_all[:, c].rearrange("p g e -> p (g e)")

            def moe(l, n_norm):
                S_, B_ = sem, lambda name: l * PER_LAYER[name]
                norm_sums(n_norm)
                pe.wait_ge(sem("h_done"), 2 * KD * (n_norm + 1))
                pe.wait_ge(sem("rout_in"), 16 * 9)
                for c in range(TC):
                    for k in range(KD):
                        last = mm(bank[0][:, c * 64:c * 64 + NG + NE], hT[:, k, c * P:(c + 1) * P], rout[:, l, k, :],
                                  start=(k == 0), stop=(k == KD - 1))
                last.then_inc(S_("logit_mm"), 1)
                for g in range(2 * TC):
                    c, hf = divmod(g, 2)
                    if g >= 2:
                        pe.wait_ge(S_(f"htok_set{g % 2}_"), B_(f"htok_set{g % 2}_") + g // 2)
                    for k in range(4):
                        last = tr(bank[4 + g % 2][:, k * P:(k + 1) * P], hT[:, 4 * hf + k, c * P:(c + 1) * P], ident)
                    last.then_inc(S_("htok_mm"), 1)
                pe.wait_ge(S_("mask_set"), B_("mask_set") + 1)
                for c in range(TC):
                    for c2 in range(c + 1):
                        last = mm(bank[1][:, c * 64:c * 64 + NE], C["before"] if c2 == c else ones,
                                  mm_mask(c2), start=(c2 == 0), stop=(c2 == c))
                for c in range(TC):
                    last = mm(bank[1][0:1, 256:256 + NE], ones[:, 0:1], mm_mask(c), start=(c == 0), stop=(c == TC - 1))
                last.then_inc(S_("place_mm"), 1)
                pe.wait_ge(S_("cum_set"), B_("cum_set") + 1)
                pe.wait_ge(S_("tab_in"), B_("tab_in") + 16)

                def turn(src, done):
                    for hf in range(2):
                        for k in range(4):
                            kk = 4 * hf + k
                            last = tr(bank[hf][:, k * P:(k + 1) * P], src[:, kk * P:(kk + 1) * P], ident)
                    last.then_inc(done, 1)

                def gate_up(gt, s, done):
                    gu = slot_gu(s)
                    for k in range(KD):
                        for j in range(2):
                            last = mm(bank[2][WIN * j:WIN * (j + 1), :], gt[:, k, WIN * j:WIN * (j + 1)], gu[:, :, j, k, :],
                                      start=(k == 0), stop=(k == KD - 1))
                    last.then_inc(done, 1)

                def turn_act(done):
                    for k in range(2):
                        last = tr(bank[3][:, k * P:(k + 1) * P], A[:, k * P:(k + 1) * P], ident)
                    last.then_inc(done, 1)

                def down(s, done):
                    dn = slot_dn(s)
                    for hf in range(2):
                        for k in range(2):
                            for j in range(2):
                                last = mm(bank[4 + hf][WIN * j:WIN * (j + 1), :], AT[:, k, WIN * j:WIN * (j + 1)],
                                          dn[:, j, k, hf * HALF:(hf + 1) * HALF], start=(k == 0), stop=(k == 1))
                    last.then_inc(done, 1)

                def extra(q, s, i):
                    apart(pe)
                    lo = pe.value_load(cumx[0:1, bass.ds(q, 1)], min_val=0, max_val=2 * PAIRS)
                    hi = pe.value_load(cumx[0:1, bass.ds(q + 1, 1)], min_val=0, max_val=2 * PAIRS)
                    with pe.If(hi > lo):
                        pe.wait_ge(S_("y_set"), B_("y_set") + 2 * q + 2)
                        pe.wait_ge(sem(f"dn_in_{s}"), B_("dn_in") + 16 * (i + 1))
                        apart(pe)
                        with pe.Fori(lo, hi) as x:
                            pe.wait_ge(S_("xgather"), 16 * (x + 1))
                            turn(Gx, S_("xturn"))
                            pe.wait_ge(S_("xgt_set"), 2 * (x + 1))
                            gate_up(GTx, s, S_("xgu_mm"))
                            pe.wait_ge(S_("xact_set"), x + 1)
                            turn_act(S_("xat_mm"))
                            pe.wait_ge(S_("xat_set"), x + 1)
                            down(s, S_("xdn_mm"))
                            pe.wait_ge(S_("xy_set"), 2 * (x + 1))

                def pair(q, s, i, final):
                    pe.wait_ge(sem(f"gu_in_{s}"), B_("gu_in") + 32 * (i + 1))
                    pe.wait_ge(S_("gt_set"), B_("gt_set") + 2 * (q + 1))
                    pe.wait_ge(S_("act_set"), B_("act_set") + q + 1)
                    extra(q, s, i)
                    gate_up(GT, s, S_("gu_mm"))
                    if not final:
                        pe.wait_ge(S_(f"gather{1 - s}_"), B_(f"gather{1 - s}_") + 16 * (i + 1 + s))
                        turn(G[:, 1 - s, :], S_("turn_mm"))
                    pe.wait_ge(S_("act_set"), B_("act_set") + q + 2)
                    turn_act(S_("at_mm"))
                    pe.wait_ge(S_("at_set"), B_("at_set") + q + 1)
                    pe.wait_ge(sem(f"dn_in_{s}"), B_("dn_in") + 16 * (i + 1))
                    pe.wait_ge(S_("y_set"), B_("y_set") + 2 * q + 2)
                    down(s, S_("dn_mm"))

                nc.tensor.nop().then_inc(S_("turn_mm"), 1)
                nc.tensor.nop().then_inc(S_("dn_mm"), 1)
                pe.wait_ge(S_("lg_set"), B_("lg_set") + 1)
                pe.wait_ge(S_("gather0_"), B_("gather0_") + 16)
                turn(G[:, 0, :], S_("turn_mm"))
                with pe.Fori(0, PAIRS // 2 - 1) as i:
                    for s in range(2):
                        pair(2 * i + s, s, i, False)
                i = PAIRS // 2 - 1
                for s in range(2):
                    pair(2 * i + s, s, i, s == 1)
                for k in range(KD):
                    if k == 0:
                        pe.wait_ge(S_("y_set"), B_("y_set") + 2 * PAIRS + 2)
                        pe.wait_ge(S_("ysum"), B_("ysum") + 1)
                    if k >= 2:
                        pe.wait_ge(S_("moe_add"), B_("moe_add") + 2 * (k - 1))
                    for c in range(TC):
                        last = tr(bank[k % 2][:, c * P:(c + 1) * P], y2[:, 0, c, k * P:(k + 1) * P], ident)
                    last.then_inc(S_("res_mm"), 1)

            moe(0, 1)

            norm_sums(2)
            pe.wait_ge(sem("h_done"), 2 * KD * 3)
            for n in range(24):
                if n % 4 == 0:
                    g = WIN_GROUP[n // 4]
                    pe.wait_ge(sem(f"win_in{g}"), 16 * WIN_GROUP.count(g))
                if n >= 2:
                    pe.wait_ge(sem("u_set"), 2 * (n - 1))
                w = win[n // 4]
                for k in range(KD):
                    last = mm(bank[n % 2][:, 0:T], w[:, k, (n % 4) * P:(n % 4 + 1) * P], hT[:, k, :],
                              start=(k == 0), stop=(k == KD - 1))
                last.then_inc(sem("hin_mm"), 1)
            for o in range(2):
                if o == 0:
                    pe.wait_ge(sem("conv_done"), 24)
                for g in range(2 * TC):
                    c, hf = divmod(g, 2)
                    g2 = 2 * TC * o + g
                    if o == 1 and g == 0:
                        pe.wait_ge(sem("gated"), 2 * KD)
                    if g2 >= 2:
                        pe.wait_ge(sem(f"ztok_set{g2 % 2}"), g2 // 2)
                    lo, hi = conv_cols(c * P, (c + 1) * P)
                    for k in range(4):
                        last = tr(bank[2 + g % 2][:, k * P:(k + 1) * P], st[:, 2, 4 * hf + k, lo:hi], ident)
                    last.then_inc(sem("ztok_mm"), 1)
                for v in range(2):
                    pe.wait_ge(sem(f"ztok_set{v}"), TC * (o + 1))
                if o == 0:
                    pe.wait_ge(sem("u_set"), 48)
                for i in range(6):
                    r, hf = divmod(i, 2)
                    g = 6 * o + i
                    if g >= 2:
                        pe.wait_ge(sem("zf_used"), g - 1)
                    for part in range(2):
                        b = bank[4 + 2 * (g % 2) + part]
                        if r < 2:
                            ops = [(C["fwd256"], c * 512 + part * 256 + r * P, 1 + c) for c in range(2)]
                        else:
                            ops = [(C["fwd128"], part * P, 0)]
                        for j, (m, off, c) in enumerate(ops):
                            last = mm(b[:, :], m[:, off:off + P], ztok[:, c, hf * HALF:(hf + 1) * HALF],
                                      start=(j == 0), stop=(j == len(ops) - 1))
                    last.then_inc(sem("zf_mm"), 1)
                pe.wait_ge(sem("cprod"), 6 * (o + 1))
                for k in range(KD):
                    g = KD * o + k
                    if g >= 2:
                        pe.wait_ge(sem("gated"), 2 * (g - 1))
                    ks = slice(k * P, (k + 1) * P)
                    for j in range(2):
                        mm(bank[g % 2][:, 0:P], Yf[:, 4 + j, ks], C["inv128"][:, j * P:(j + 1) * P],
                           start=(j == 0), stop=(j == 1))
                    for j in range(4):
                        last = mm(bank[g % 2][:, P:T], Yf[:, j, ks], C["inv256"][:, j * DEC:(j + 1) * DEC],
                                  start=(j == 0), stop=(j == 3))
                    last.then_inc(sem("inv_mm"), 1)
            pe.wait_ge(sem("wout_in"), 16)
            pe.wait_ge(sem("gated"), 4 * KD)
            for m in range(KD):
                if m >= 2:
                    pe.wait_ge(sem("mix1_done"), 2 * (m - 1))
                for lo, hi in SPANS:
                    a0, a1 = conv_cols(lo, hi)
                    for k in range(KD):
                        last = mm(bank[2 + m % 2][:, lo:hi], wout[:, k, m * P:(m + 1) * P], st[:, 2, k, a0:a1],
                                  start=(k == 0), stop=(k == KD - 1))
                last.then_inc(sem("mix1_mm"), 1)
            pe.wait_ge(sem("mix1_done"), 2 * KD)
            moe(1, 3)

            norm_sums(4)
            pe.wait_ge(sem("h_done"), 2 * KD * 4 + KD)
            for g in range(2 * TC):
                c, hf = divmod(g, 2)
                if g >= 2:
                    pe.wait_ge(sem("yout_done"), g - 1)
                for k in range(4):
                    last = tr(bank[4 + g % 2][:, k * P:(k + 1) * P], hT[:, 4 * hf + k, c * P:(c + 1) * P], ident)
                last.then_inc(sem("yout_mm"), 1)

        def qk_root(act, fn, m):
            act.wait_ge(sem("qss_mm"), m + 1)
            if m >= 2:
                act.wait_ge(sem("qn_set"), m - 1)
            fn(rq[:, m % 2, :], bank[4 + m % 2][:, 0:T], ACT.Sqrt, scale=1.0 / HD, bias=eps_col[:, 0:1])\
                .then_inc(sem("qrt_set"), 1)

        @block.scalar
        def _(act):
            fn = nc.scalar.activation

            act.wait_ge(sem("preset"), 3)
            act.wait_ge(sem("pc_done"), 1)
            fn(condS[:, :, 0], pc[:, R_CCTX:R_CCTX + KD], ACT.Silu).then_inc(sem("cond_set"), 1)
            fn(condS[:, :, 1], pc[:, R_C:R_C + KD], ACT.Silu).then_inc(sem("cond_set"), 1)
            for i in range(2):
                act.wait_ge(sem("angle_set"), i + 1)
                fn(hd1[0:FH, i, :], hdr[0:FH, i, :], ACT.Sin).then_inc(sem("mlp_done"), 1)

            def adaR_copy(t):
                act.wait_ge(sem("ada_mm"), t + 1)
                if t >= 2:
                    act.wait_ge(sem("ada_tr"), t - 1)
                fn(adaR[:, t % 2, :], bank[t % 2][:, 0:256], ACT.Copy).then_inc(sem("adaR_set"), 1)

            def filters(f):
                act.wait_ge(sem(f"decay_in{f % 2}"), 32 * (f // 2 + 1))
                for d in range(2):
                    fn(eld[:, f % 2, d, :], eld[:, f % 2, d, :], ACT.Exp).then_inc(sem("rate_set"), 1)
                act.wait_ge(sem("rate_set"), 2 * (f + 1))
                for i in range(7):
                    g = 6 * f + i
                    d, c = divmod(i, 3)
                    if i < 6:
                        if g >= 2:
                            act.wait_ge(sem("taps_done"), g - 1)
                        fn(dec[:, g % 2, :], eld[:, f % 2, d, :], ACT.Exp, scale=C["tneg"][:, c:c + 1])\
                            .then_inc(sem("dec_set"), 1)
                    if i >= 1:
                        g, (d, c) = g - 1, divmod(i - 1, 3)
                        act.wait_ge(sem("taps_done"), g + 1)
                        if g >= 2:
                            act.wait_ge(sem("size_mm"), g - 1)
                        fn(absb[:, g % 2, :], hfb[:, d, c, :], ACT.Abs).then_inc(sem("abs_done"), 1)
                for i in range(6):
                    g = 6 * f + i
                    act.wait_ge(sem("cf_set"), g + 1)
                    o, n = FILT[f]
                    act.dma_start(cfD[o][:, i, n * HALF:(n + 1) * HALF], cfb[:, i, :]).then_inc(sem("cf_out"), 16)

            for t in range(NADA):
                adaR_copy(t)
                if t in FILT_AFTER:
                    filters(FILT_AFTER[t])

            def squares(n):
                for k in range(KD):
                    g = KD * n + k
                    act.wait_ge(sem("x_ready"), g + 1)
                    if g >= 2:
                        act.wait_ge(sem("sq_mm"), g - 1)
                    fn(sq[:, k % 2, :], xT[:, k, :], ACT.Square).then_inc(sem("sq_done"), 1)
                act.wait_ge(sem("sq_mm"), KD * (n + 1))
                fn(rstd[:, :], bank[3][:, 0:T], ACT.Sqrt, scale=1.0 / D, bias=eps_col[:, 0:1]).then_inc(sem("rt_done"), 1)

            def modulate(n, l, which):
                for k in range(KD):
                    act.wait_ge(sem("xn_set"), KD * n + k + 1)
                    for c, (lo, hi) in enumerate(SPANS):
                        fn(hT[:, k, lo:hi], hT[:, k, lo:hi], ACT.Identity, scale=amul[:, l, which, k, c:c + 1],
                           bias=ada[:, l, 3 * which, k, c:c + 1]).then_inc(sem("h_done"), 1)

            act.wait_ge(sem("ada_tr"), NADA)
            squares(0)
            modulate(0, 0, 0)
            for m in range(QK):
                act.wait_ge(sem("qk_mm"), m + 1)
                if m >= 2:
                    act.wait_ge(sem("qss_mm"), m - 1)
                fn(sq[:, m % 2, :], bank[m % 2][:, 0:T], ACT.Square).then_inc(sem("qsq_set"), 1)
                if m >= 1:
                    qk_root(act, fn, m - 1)
            qk_root(act, fn, QK - 1)
            for c in range(TC):
                act.wait_ge(sem("v_mm"), c + 1)
                fn(V[:, c, :], bank[c % 2][:, 0:256], ACT.Copy).then_inc(sem("v_done"), 1)
            act.wait_ge(sem("ktok_mm"), 1)
            fn(ktok, bank[7][:, 0:256], ACT.Copy).then_inc(sem("ktok_done"), 1)

            def exps(n):
                act.wait_ge(sem("nb_set"), n + 1)
                if n >= 2:
                    act.wait_ge(sem("probT_mm"), n - 1)
                X, Z = bank[2 * (n % 2)], bank[2 * (n % 2) + 1]
                for i, src in enumerate((X[:, 0:T], Z[:, 0:T], Z[:, T:512])):
                    dst = prob[:, n % 2, i * T:i * T + (T if i < 2 else P)]
                    fn(dst, src, ACT.Exp, scale=HD ** -0.5, bias=nb[:, n % 2, i:i + 1],
                       accum_out=rsum[:, n % 2, i:i + 1]).then_inc(sem("exp_done"), 1)

            for n in range(NH + 1):
                if n < NH:
                    exps(n)
                if n >= 1:
                    j = n - 1
                    act.wait_ge(sem("probT_mm"), j + 1)
                    if j >= 2:
                        act.wait_ge(sem("oT_mm"), j - 1)
                    fn(probT[:, j % 2, 0:512], bank[4][:, :], ACT.Copy).then_inc(sem("probTa_set"), 1)

            def moe(l, n_norm):
                S_, B_ = sem, lambda name: l * PER_LAYER[name]
                squares(n_norm)
                modulate(n_norm, l, 1)
                act.wait_ge(S_("gsub_set"), B_("gsub_set") + 1)
                fn(gx.rearrange("p a b -> p (a b)"), gx.rearrange("p a b -> p (a b)"), ACT.Exp).then_inc(S_("gexp"), 1)
                act.wait_ge(S_("dv_set"), B_("dv_set") + 1)
                fn(ev.rearrange("p a b -> p (a b)"), ev.rearrange("p a b -> p (a b)"), ACT.Exp).then_inc(S_("gexp"), 1)

                def extra(q):
                    lo = act.value_load(cumx[0:1, bass.ds(q, 1)], min_val=0, max_val=2 * PAIRS)
                    hi = act.value_load(cumx[0:1, bass.ds(q + 1, 1)], min_val=0, max_val=2 * PAIRS)
                    with act.If(hi > lo):
                        with act.Fori(lo, hi) as x:
                            act.wait_ge(S_("xturn"), x + 1)
                            fn(GTx[:, 0:4, :], bank[0].rearrange("p (k s) -> p k s", k=4), ACT.Copy).then_inc(S_("xgt_set"), 1)
                            act.wait_ge(S_("xgu_mm"), x + 1)
                            fn(S, bank[2][:, 0:EH], ACT.Silu).then_inc(S_("xsilu"), 1)
                            act.wait_ge(S_("xdn_mm"), x + 1)
                            act.wait_ge(S_("xy_free"), x + 1)
                            fn(Yx[:, 0:HALF], bank[4][:, :], ACT.Copy).then_inc(S_("xy_set"), 1)

                def turn_copy(q):
                    act.wait_ge(S_("turn_mm"), B_("turn_mm") + q + 2)
                    fn(GT[:, 0:4, :], bank[0].rearrange("p (k s) -> p k s", k=4), ACT.Copy).then_inc(S_("gt_set"), 1)

                def pair(q, s, final):
                    extra(q)
                    act.wait_ge(S_("gu_mm"), B_("gu_mm") + q + 1)
                    fn(S, bank[2][:, 0:EH], ACT.Silu).then_inc(S_("silu"), 1)
                    if not final:
                        turn_copy(q + 1)
                    act.wait_ge(S_("dn_mm"), B_("dn_mm") + q + 2)
                    act.wait_ge(S_("y_free"), B_("y_free") + q + 1)
                    fn(Y[:, s, 0:HALF], bank[4][:, :], ACT.Copy).then_inc(S_("y_set"), 1)

                act.wait_ge(S_("cum_set"), B_("cum_set") + 1)
                nc.scalar.nop().then_inc(S_("y_set"), 1)
                turn_copy(0)
                with act.Fori(0, PAIRS // 2 - 1) as i:
                    for s in range(2):
                        pair(2 * i + s, s, False)
                for s in range(2):
                    pair(PAIRS - 2 + s, s, s == 1)

            moe(0, 1)
            squares(2)
            modulate(2, 1, 0)
            for n in range(24):
                stream, k = divmod(WIN_ORDER[n // 4] * 4 + n % 4, KD)
                act.wait_ge(sem("hin_mm"), n + 1)
                if n >= 2:
                    act.wait_ge(sem("conv_done"), n - 1)
                else:
                    act.wait_ge(sem("upad_clear"), 1)
                r = R_BIN + stream * KD + k
                for lo, hi in SPANS:
                    a0, a1 = conv_cols(lo, hi)
                    fn(upad[:, n % 2, a0 + 1:a1 + 1], bank[n % 2][:, lo:hi], ACT.Identity, bias=pc[:, r:r + 1])\
                        .then_inc(sem("u_set"), 1)
            for o in range(2):
                for g in range(0, 2 * TC, 2):
                    c, hf = divmod(g, 2)
                    act.wait_ge(sem("ztok_mm"), 2 * TC * o + g + 1)
                    if g == 0:
                        act.wait_ge(sem("hin_mm"), 24)
                    fn(ztok[:, c, 0:HALF], bank[2][:, :], ACT.Copy).then_inc(sem("ztok_set0"), 1)
            moe(1, 3)
            squares(4)
            for k in range(KD):
                act.wait_ge(sem("xn_set"), KD * 4 + k + 1)
                fn(hT[:, k, :], hT[:, k, :], ACT.Copy, scale=pc[:, R_FIN + k:R_FIN + k + 1]).then_inc(sem("h_done"), 1)

        @block.vector
        def _(dve):
            v = nc.vector
            chain = [0]

            def link(ins):
                chain[0] += 1
                ins.then_inc(sem("dve_chain"), 1)
                dve.wait_ge(sem("dve_chain"), chain[0])

            v.memset(none_tile, NONE).then_inc(sem("preset"), 1)
            v.memset(condS[:, :, :], 0.0).then_inc(sem("preset"), 1)
            v.memset(eps_col[:, :], EPS).then_inc(sem("preset"), 1)
            dve.wait_ge(sem("pc_mm"), 1)
            v.tensor_copy(pc[:, :], bank[7][:, 0:R_END]).then_inc(sem("pc_done"), 1)
            for k in range(KD):
                dve.wait_ge(sem("xT_mm"), k + 1)
                v.tensor_copy(xT[:, k, :], bank[k % 4][:, 0:T]).then_inc(sem("xT_done"), 1)
            dve.wait_ge(sem("xT_done"), KD)
            nc.vector.nop().then_inc(sem("x_ready"), KD)

            TURN = 2 * np.pi
            HI = float(np.float32(6.28125))
            LO = float(np.float32(TURN - 6.28125))
            BIG = float(1.5 * 2 ** 23)
            for i in range(2):
                dve.wait_ge(sem("mlp_mm"), i + 1)
                x, t = hdr[0:FH, i, :], hdt[0:FH, :]
                link(v.tensor_scalar(x, bank[4 + i][0:FH, 0:T], fcol[:, i:i + 1], fcol[:, 2:3], ALU.add, ALU.mult))
                link(v.tensor_scalar(t, x, float(1 / TURN), BIG, ALU.mult, ALU.add))
                link(v.tensor_scalar(t, t, BIG, None, ALU.subtract))
                link(v.scalar_tensor_tensor(x, t, -HI, x, ALU.mult, ALU.add))
                link(v.scalar_tensor_tensor(x, t, -LO, x, ALU.mult, ALU.add))
                if i == 1:
                    link(v.memset(hd1[FH:FH + 1, 1, :], 1.0))
                v.tensor_scalar(x, x, PI_F, -PI_F, ALU.min, ALU.max).then_inc(sem("angle_set"), 1)

            def ada_add(t):
                l, s = divmod(t, 6)
                dve.wait_ge(sem("ada_tr"), t + 1)
                for u in range(2):
                    src = bank[2][:, u * P:(u + 1) * P].rearrange("p (j c) -> p j c", j=4)[:, :, 0:2]
                    dst = ada[:, l, s].rearrange("p (j u) c -> p u j c", u=2)[:, u]
                    r = R_BADA + l * 48 + s * KD
                    bia = pc[:, r:r + KD].rearrange("p (j u a) -> p u j a", u=2, a=1)[:, u].to_broadcast([P, 4, 2])
                    last = v.tensor_tensor(dst, src, bia, ALU.add)
                last.then_inc(sem("ada_done"), 1)

            def filters(f):
                for i in range(6):
                    g = 6 * f + i
                    d, c = divmod(i, 3)
                    dve.wait_ge(sem("taps_mm"), g + 1)
                    dve.wait_ge(sem("dec_set"), g + 1)
                    if i == 0 and f > 0:
                        dve.wait_ge(sem("abs_done"), 6 * f)
                        dve.wait_ge(sem("smdf_done"), 6 * f)
                        dve.wait_ge(sem("cf_mm"), 6 * f)
                    v.tensor_tensor(hfb[:, d, c, :], bank[4 + g % 2][:, :], dec[:, g % 2, :], ALU.mult)\
                        .then_inc(sem("taps_done"), 1)
                dve.wait_ge(sem("taps_done"), 6 * (f + 1))
                if f > 0:
                    dve.wait_ge(sem("cf_mm"), 6 * f)
                    dve.wait_ge(sem("cf_set"), 6 * f)
                for d in range(2):
                    for c in range(3):
                        v.tensor_tensor(smdf[:, d, c, :], hfb[:, 0, c, :], hfb[:, 1, c, :], ALU.subtract if d else ALU.add)\
                            .then_inc(sem("smdf_done"), 1)
                dve.wait_ge(sem("size_mm"), 6 * (f + 1))
                for b in range(2):
                    link(v.tensor_scalar(rn[:, b, :], bank[6 + b][:, :], EPS, None, ALU.add))
                    v.reciprocal(rn[:, b, :], rn[:, b, :]).then_inc(sem("rn_set"), 1)
                dve.wait_ge(sem("rn_set"), 2 * (f + 1))
                for i in range(6):
                    g = 6 * f + i
                    dve.wait_ge(sem("cf_mm"), g + 1)
                    if f > 0:
                        dve.wait_ge(sem("cf_out"), 16 * 6 * f)
                    v.tensor_tensor(cfb[:, i, :], bank[4 + g % 2][:, :], rn[:, 0 if i >= 4 else 1, :], ALU.mult)\
                        .then_inc(sem("cf_set"), 1)

            for t in range(NADA):
                if t >= 1:
                    ada_add(t - 1)
                if t in FILT_AFTER:
                    filters(FILT_AFTER[t])
            ada_add(NADA - 1)
            dve.wait_ge(sem("ada_done"), NADA)
            for l in range(DEPTH):
                for w, r0 in ((0, R_NMIX), (1, R_NFFN)):
                    gain = pc[:, r0 + l * KD:r0 + (l + 1) * KD].rearrange("p (k a) -> p k a", a=1).to_broadcast([P, KD, 2])
                    link(v.scalar_tensor_tensor(amul[:, l, w], ada[:, l, 3 * w + 1], 1.0, gain, ALU.add, ALU.mult))
            bo = pc[:, R_BOUT:R_BOUT + KD].rearrange("p (k a) -> p k a", a=1).to_broadcast([P, KD, 2])
            link(v.tensor_tensor(gbo[:, :, :], ada[:, 1, 2], bo, ALU.mult))

            def norm(n):
                dve.wait_ge(sem("rt_done"), n + 1)
                link(v.reciprocal(rstd[:, :], rstd[:, :]))
                for k in range(KD):
                    v.tensor_tensor(hT[:, k, :], xT[:, k, :], rstd[:, :], ALU.mult).then_inc(sem("xn_set"), 1)

            def add_mix(src_of, done, g, mmsem, base=0):
                for k in range(KD):
                    dve.wait_ge(mmsem, base + k + 1)
                    for c, (lo, hi) in enumerate(SPANS):
                        v.scalar_tensor_tensor(xT[:, k, lo:hi], src_of(k)[:, lo:hi], g[:, k, c:c + 1], xT[:, k, lo:hi],
                                               ALU.mult, ALU.add).then_inc(done, 1)

            dve.wait_ge(sem("cf_out"), 16 * 24)
            norm(0)
            def qk_norm(m):
                dve.wait_ge(sem("qrt_set"), m + 1)
                link(v.reciprocal(rq[:, m % 2, :], rq[:, m % 2, :]))
                dve.wait_ge(sem("raw_set"), m + 1)
                v.tensor_tensor(chunk_dst(m, 0, T), raw[:, m % 2, :], rq[:, m % 2, :], ALU.mult).then_inc(sem("qn_set"), 1)

            dve.wait_ge(sem("cache_in"), 48)

            def qk_turn(m):
                dve.wait_ge(sem("rot_mm"), m + 1)
                if m >= 2:
                    dve.wait_ge(sem("qk_done"), m - 1)
                v.tensor_tensor(rs_[:, m % 2, :], bank[6 + m % 2][:, 0:DEC], C["sin"], ALU.mult).then_inc(sem("qs_set"), 1)
                x = chunk_dst(m, SEQ, T)
                link(v.tensor_tensor(x, x, C["cos"], ALU.mult))
                dve.wait_ge(sem("qs_set"), m + 1)
                v.tensor_tensor(x, x, rs_[:, m % 2, :], ALU.add).then_inc(sem("qk_done"), 1)

            for m in range(QK + 2):
                if m < QK:
                    dve.wait_ge(sem("qsq_set"), m + 1)
                    if m >= 2:
                        dve.wait_ge(sem("qn_set"), m - 1)
                    gain = pc[:, R_KN:R_KN + 1] if m < 2 else pc[:, R_QN:R_QN + 1]
                    v.tensor_scalar(raw[:, m % 2, :], bank[m % 2][:, 0:T], gain, None, ALU.mult).then_inc(sem("raw_set"), 1)
                if 1 <= m <= QK:
                    qk_norm(m - 1)
                if m >= 2:
                    qk_turn(m - 2)
            dve.wait_ge(sem("ck_mm"), 1)
            v.tensor_copy(kT[:, :, T:512], bank[6][:, 0:256].rearrange("p (c t) -> p c t", c=2)).then_inc(sem("ck_set"), 1)

            def maxima(n):
                dve.wait_ge(sem("score_mm"), n + 1)
                X, Z = bank[2 * (n % 2)], bank[2 * (n % 2) + 1]
                for i, src in enumerate((X[:, 0:T], Z[:, 0:T], Z[:, T:512])):
                    last = v.reduce_max(mx[:, n % 2, i:i + 1], src, axis=AX.X)
                    link(last)
                v.tensor_scalar(nb[:, n % 2, :], mx[:, n % 2, :], -(HD ** -0.5), None, ALU.mult).then_inc(sem("nb_set"), 1)

            def probs(n):
                dve.wait_ge(sem("exp_done"), 3 * (n + 1))
                link(v.reciprocal(rinv[:, n % 2, :], rsum[:, n % 2, :]))
                for i in range(3):
                    x = prob[:, n % 2, i * T:i * T + (T if i < 2 else P)]
                    last = v.tensor_scalar(x, x, rinv[:, n % 2, i:i + 1], None, ALU.mult)
                    last.then_inc(sem("prob_done"), 1)

            for n in range(NH + 2):
                if n < NH:
                    maxima(n)
                if 1 <= n <= NH:
                    probs(n - 1)
                if n >= 1 and n <= NH:
                    j = n - 1
                    dve.wait_ge(sem("probT_mm"), j + 1)
                    if j >= 2:
                        dve.wait_ge(sem("oT_mm"), j - 1)
                    v.tensor_copy(probT[:, j % 2, 512:896], bank[5][:, 0:T]).then_inc(sem("probTb_set"), 1)
                if n >= 2 and n % 2 == 1:
                    c = (n - 2) // 2
                    dve.wait_ge(sem("oT_mm"), 2 * (c + 1))
                    v.tensor_copy(oT[:, c, :], bank[6 + c % 2][:, 0:T]).then_inc(sem("oT_set"), 1)
            add_mix(lambda k: bank[k % 2], sem("mix0_done"), ada[:, 0, 2], sem("mix0_mm"))
            dve.wait_ge(sem("mix0_done"), 2 * KD)
            nc.vector.nop().then_inc(sem("x_ready"), KD)

            def bc(x, *shape):
                return x.to_broadcast(list(shape))

            def router(l):
                S_, B_ = sem, lambda name: l * PER_LAYER[name]
                dve.wait_ge(S_("logit_mm"), B_("logit_mm") + 1)
                src = bank[0][:, 0:TC * 64].rearrange("p (c e) -> p c e", c=TC)[:, :, 0:NG + NE]
                bias = rbias[:, l:l + 1, :].to_broadcast([P, TC, NG + NE])
                v.tensor_tensor(lg, src, bias, ALU.add).then_inc(S_("lg_set"), 1)
                dve.wait_ge(S_("lg_set"), B_("lg_set") + 1)
                g_ = lg[:, :, 0:NG]
                pr_g = C["prio"][:, 0:NG].rearrange("p (a g) -> p a g", a=1).to_broadcast([P, TC, NG])
                pr_e = C["prio"][:, NG:NG + EG].rearrange("p (a g) -> p a g", a=1).to_broadcast([P, TC, EG])
                link(v.reduce_max(gmax, g_, axis=AX.X))
                v.tensor_tensor(gx, g_, bc(gmax, P, TC, NG), ALU.subtract).then_inc(S_("gsub_set"), 1)
                first(g_, gmax, geq, v2, goh, pr_g, NG)
                for g in range(NG):
                    e_ = lg[:, :, NG + g * EG:NG + (g + 1) * EG]
                    if g == 0:
                        link(v.tensor_tensor(esel, e_, bc(goh[:, :, 0:1], P, TC, EG), ALU.mult))
                    else:
                        link(v.tensor_tensor(etmp, e_, bc(goh[:, :, g:g + 1], P, TC, EG), ALU.mult))
                        link(v.tensor_tensor(esel, esel, etmp, ALU.add))
                link(v.reduce_max(v1, esel, axis=AX.X))
                first(esel, v1, eeq, den, oh1, pr_e, EG)
                link(v.tensor_scalar(etmp, oh1, -3.0e38, None, ALU.mult))
                link(v.tensor_scalar(e2, oh1, -1.0, 1.0, ALU.mult, ALU.add))
                link(v.tensor_tensor(e2, esel, e2, ALU.mult))
                link(v.tensor_tensor(e2, e2, etmp, ALU.add))
                link(v.reduce_max(v2, e2, axis=AX.X))
                first(e2, v2, eeq, den, oh2, pr_e, EG)
                v.tensor_tensor(ev, v2, v1, ALU.subtract).then_inc(S_("dv_set"), 1)
                for m_, oh in ((m1, oh1), (m2, oh2)):
                    for c in range(TC):
                        go = goh[:, c, :].rearrange("p (g a) -> p g a", a=1).to_broadcast([P, NG, EG])
                        eo = oh[:, c, :].rearrange("p (a e) -> p a e", a=1).to_broadcast([P, NG, EG])
                        link(v.tensor_tensor(m_[:, c], go, eo, ALU.mult))
                v.tensor_tensor(m_all, m1, m2, ALU.add).then_inc(S_("mask_set"), 1)
                dve.wait_ge(S_("gexp"), B_("gexp") + 2)
                link(v.reduce_sum(gden, gx, axis=AX.X))
                link(v.tensor_scalar(den, ev, 1.0, None, ALU.add))
                link(v.tensor_tensor(den, den, gden, ALU.mult))
                link(v.reciprocal(wck[:, :, 0:1], den))
                link(v.tensor_tensor(wck[:, :, 1:2], wck[:, :, 0:1], ev, ALU.mult))
                dve.wait_ge(S_("place_mm"), B_("place_mm") + 1)
                place = bank[1][:, 0:TC * 64].rearrange("p (c e) -> p c e", c=TC)[:, :, 0:NE]
                base = C["rowbase"].rearrange("p (a e) -> p a e", a=1).to_broadcast([P, TC, NE])
                for k, m_ in enumerate((m1, m2)):
                    mf = m_.rearrange("p c g e -> p c (g e)")
                    link(v.tensor_tensor(mtmp, place, mf, ALU.mult))
                    link(v.reduce_sum(posk[:, :, k:k + 1], mtmp, axis=AX.X))
                    link(v.tensor_tensor(mtmp, base, mf, ALU.mult))
                    link(v.reduce_sum(basek[:, :, k:k + 1], mtmp, axis=AX.X))
                link(v.scalar_tensor_tensor(rowk, posk, float(PAIRS), basek, ALU.mult, ALU.add))
                for w in range(1, NWIN):
                    link(v.tensor_scalar(basek, posk, float(w * WIN), float(WIN * PAIRS), ALU.is_ge, ALU.mult))
                    link(v.tensor_tensor(rowk, rowk, basek, ALU.add))
                link(v.tensor_copy(idx[:, :], rowk.rearrange("p a b -> p (a b)")))
                link(v.tensor_copy(pay[:, :, :, :].rearrange("p a b c -> p (a b c)"), trow[:, :]))
                v.tensor_copy(pay[:, :, :, 2].bitcast(F32), wck).then_inc(S_("slots_set"), 1)
                c0, c1, c2 = cnt[:, 0:NE], cnt[:, 32:49], cnt[:, 64:81]
                link(v.memset(c1, 0.0))
                if l > 0:
                    link(v.tensor_copy(c1[:, 0:1], cumx[:, PAIRS:PAIRS + 1]))
                link(v.tensor_copy(c0, bank[1][0:1, 256:256 + NE]))
                pr = c0.rearrange("p (q j) -> p q j", j=2)
                link(v.tensor_tensor(cnt[:, 96:112], pr[:, :, 0], pr[:, :, 1], ALU.max))
                for w in range(1, NWIN):
                    link(v.tensor_scalar(c2[:, 0:PAIRS], cnt[:, 96:112], float(w * WIN), None, ALU.is_gt))
                    link(v.tensor_tensor(c1[:, 1:PAIRS + 1], c1[:, 1:PAIRS + 1], c2[:, 0:PAIRS], ALU.add))
                src_, dst_ = c1, c2
                for sh in (1, 2, 4, 8):
                    link(v.tensor_copy(dst_[:, 0:sh], src_[:, 0:sh]))
                    link(v.tensor_tensor(dst_[:, sh:PAIRS + 1], src_[:, sh:PAIRS + 1], src_[:, 0:PAIRS + 1 - sh], ALU.add))
                    src_, dst_ = dst_, src_
                v.tensor_copy(cumx[:, :], src_).then_inc(S_("cum_set"), 1)

            def first(x, top, eq, key, oh, prio, n):
                link(v.tensor_tensor(eq, x, bc(top, P, TC, n), ALU.is_equal))
                link(v.tensor_tensor(eq, eq, prio, ALU.mult))
                link(v.reduce_max(key, eq, axis=AX.X))
                link(v.tensor_tensor(oh, eq, bc(key, P, TC, n), ALU.is_equal))

            def moe(l, n_norm):
                S_, B_ = sem, lambda name: l * PER_LAYER[name]
                norm(n_norm)
                router_and_rows(l)

                def extra(q):
                    lo = dve.value_load(cumx[0:1, bass.ds(q, 1)], min_val=0, max_val=2 * PAIRS)
                    hi = dve.value_load(cumx[0:1, bass.ds(q + 1, 1)], min_val=0, max_val=2 * PAIRS)
                    with dve.If(hi > lo):
                        with dve.Fori(lo, hi) as x:
                            dve.wait_ge(S_("xturn"), x + 1)
                            v.tensor_copy(GTx[:, 4:8, :], bank[1].rearrange("p (k s) -> p k s", k=4)).then_inc(S_("xgt_set"), 1)
                            dve.wait_ge(S_("xsilu"), x + 1)
                            v.scalar_tensor_tensor(A, bank[2][:, EH:2 * EH], curx[:, 2:3].bitcast(F32), S, ALU.mult, ALU.mult)\
                                .then_inc(S_("xact_set"), 1)
                            dve.wait_ge(S_("xat_mm"), x + 1)
                            v.tensor_copy(AT, bank[3][:, 0:256].rearrange("p (k s) -> p k s", k=2)).then_inc(S_("xat_set"), 1)
                            dve.wait_ge(S_("xdn_mm"), x + 1)
                            dve.wait_ge(S_("xy_free"), x + 1)
                            v.tensor_copy(Yx[:, HALF:D], bank[5][:, :]).then_inc(S_("xy_set"), 1)

                def turn_copy(q):
                    dve.wait_ge(S_("turn_mm"), B_("turn_mm") + q + 2)
                    v.tensor_copy(GT[:, 4:8, :], bank[1].rearrange("p (k s) -> p k s", k=4)).then_inc(S_("gt_set"), 1)

                def pair(q, s, final):
                    extra(q)
                    dve.wait_ge(S_("silu"), B_("silu") + q + 1)
                    v.scalar_tensor_tensor(A, bank[2][:, EH:2 * EH], cur[:, s, 2:3].bitcast(F32), S, ALU.mult, ALU.mult)\
                        .then_inc(S_("act_set"), 1)
                    if not final:
                        turn_copy(q + 1)
                    dve.wait_ge(S_("at_mm"), B_("at_mm") + q + 1)
                    v.tensor_copy(AT, bank[3][:, 0:256].rearrange("p (k s) -> p k s", k=2)).then_inc(S_("at_set"), 1)
                    dve.wait_ge(S_("dn_mm"), B_("dn_mm") + q + 2)
                    dve.wait_ge(S_("y_free"), B_("y_free") + q + 1)
                    v.tensor_copy(Y[:, s, HALF:D], bank[5][:, :]).then_inc(S_("y_set"), 1)

                nc.vector.nop().then_inc(S_("act_set"), 1)
                nc.vector.nop().then_inc(S_("y_set"), 1)
                turn_copy(0)
                with dve.Fori(0, PAIRS // 2 - 1) as i:
                    for s in range(2):
                        pair(2 * i + s, s, False)
                for s in range(2):
                    pair(PAIRS - 2 + s, s, s == 1)
                dve.wait_ge(S_("y2_in"), B_("y2_in") + 32)
                v.tensor_tensor(y2[:, 0].rearrange("p c d -> p (c d)"), y2[:, 0].rearrange("p c d -> p (c d)"),
                                y2[:, 1].rearrange("p c d -> p (c d)"), ALU.add).then_inc(S_("ysum"), 1)
                add_mix(lambda k: bank[k % 2], S_("moe_add"), ada[:, l, 5], S_("res_mm"), B_("res_mm"))
                dve.wait_ge(S_("moe_add"), B_("moe_add") + 2 * KD)
                nc.vector.nop().then_inc(sem("x_ready"), KD)

            def router_and_rows(l):
                S_, B_ = sem, lambda name: l * PER_LAYER[name]
                if l == 0:
                    dve.wait_ge(sem("kv_out"), 32)
                for g in range(2 * TC):
                    c, hf = divmod(g, 2)
                    dve.wait_ge(S_("htok_mm"), B_("htok_mm") + g + 1)
                    dst = hTok[:, c, :].rearrange("p (k a) -> p a k", k=8)[:, 64 * hf:64 * (hf + 1), :]
                    v.tensor_copy(dst, bank[4 + g % 2].rearrange("p (a k) -> p a k", k=8)).then_inc(S_(f"htok_set{g % 2}_"), 1)
                v.memset(G[:, :, :], 0.0).then_inc(S_("g_clear"), 1)
                v.memset(Gx, 0.0).then_inc(S_("g_clear"), 1)
                router(l)

            moe(0, 1)
            norm(2)
            v.memset(upad[:, :, :], 0.0).then_inc(sem("upad_clear"), 1)
            for n in range(24):
                stream, k = divmod(WIN_ORDER[n // 4] * 4 + n % 4, KD)
                dve.wait_ge(sem("u_set"), 2 * (n + 1))
                if n >= 2:
                    dve.wait_ge(sem("conv_done"), n - 1)
                u, t = upad[:, n % 2, :], cv[:, n % 2, :]
                w = lambda i: pc[:, R_SW + i * 24 + stream * KD + k:R_SW + i * 24 + stream * KD + k + 1]
                r = R_SB + stream * KD + k
                link(v.tensor_scalar(t, u[:, 0:UW], w(0), pc[:, r:r + 1], ALU.mult, ALU.add))
                link(v.scalar_tensor_tensor(t, u[:, 1:UW + 1], w(1), t, ALU.mult, ALU.add))
                v.scalar_tensor_tensor(st[:, stream, k, :], u[:, 2:UW + 2], w(2), t, ALU.mult, ALU.add)\
                    .then_inc(sem("conv_done"), 1)
            for o in range(2):
                for g in range(1, 2 * TC, 2):
                    c, hf = divmod(g, 2)
                    dve.wait_ge(sem("ztok_mm"), 2 * TC * o + g + 1)
                    v.tensor_copy(ztok[:, c, HALF:D], bank[3][:, :]).then_inc(sem("ztok_set1"), 1)
                dve.wait_ge(sem(f"cf_in{o}"), 16)
                for i in range(6):
                    r, hf = divmod(i, 2)
                    g = 6 * o + i
                    hs = slice(hf * HALF, (hf + 1) * HALF)
                    re, im = (r, 2 + r) if r < 2 else (4, 5)
                    dve.wait_ge(sem("zf_mm"), g + 1)
                    if o == 1 and i == 0:
                        dve.wait_ge(sem("inv_mm"), KD)
                    zr, zi = bank[4 + 2 * (g % 2)][:, :], bank[5 + 2 * (g % 2)][:, :]
                    rr, ii, ri, ir = [prod[:, j, :] for j in range(4)]
                    link(v.tensor_tensor(rr, zr, cf[:, re, hs], ALU.mult))
                    link(v.tensor_tensor(ii, zi, cf[:, im, hs], ALU.mult))
                    link(v.tensor_tensor(ri, zr, cf[:, im, hs], ALU.mult))
                    link(v.tensor_tensor(ir, zi, cf[:, re, hs], ALU.mult))
                    nc.vector.nop().then_inc(sem("zf_used"), 1)
                    link(v.tensor_tensor(Yf[:, im, hs], ri, ir, ALU.add))
                    if r != 1:
                        link(v.tensor_copy(Yf[0:1, im, hs], ii[0:1, :]))
                        link(v.memset(ii[0:1, :], 0.0))
                    link(v.tensor_tensor(Yf[:, re, hs], rr, ii, ALU.subtract))
                    nc.vector.nop().then_inc(sem("cprod"), 1)
                for k in range(KD):
                    g = KD * o + k
                    dve.wait_ge(sem("inv_mm"), g + 1)
                    sk = pc[:, R_SKIP + o * KD + k:R_SKIP + o * KD + k + 1]
                    if g >= 1:
                        dve.wait_ge(sem("gated"), 2 * g)
                    for lo, hi in SPANS:
                        a0, a1 = conv_cols(lo, hi)
                        link(v.scalar_tensor_tensor(ztmp[:, lo:hi], st[:, 2, k, a0:a1], sk, bank[g % 2][:, lo:hi],
                                                    ALU.mult, ALU.add))
                        v.tensor_tensor(st[:, 2, k, a0:a1], ztmp[:, lo:hi], st[:, o, k, a0:a1], ALU.mult)\
                            .then_inc(sem("gated"), 1)
                dve.wait_ge(sem("gated"), 2 * KD * (o + 1))
            for k in range(KD):
                dve.wait_ge(sem("mix1_mm"), k + 1)
                if k >= 1:
                    dve.wait_ge(sem("mix1_done"), 2 * k)
                for c, (lo, hi) in enumerate(SPANS):
                    link(v.tensor_scalar(ytmp[:, lo:hi], bank[2 + k % 2][:, lo:hi], ada[:, 1, 2, k, c:c + 1], gbo[:, k, c:c + 1],
                                         ALU.mult, ALU.add))
                    v.tensor_tensor(xT[:, k, lo:hi], xT[:, k, lo:hi], ytmp[:, lo:hi], ALU.add).then_inc(sem("mix1_done"), 1)
            dve.wait_ge(sem("mix1_done"), 2 * KD)
            nc.vector.nop().then_inc(sem("x_ready"), KD)
            moe(1, 3)
            norm(4)
            for g in range(2 * TC):
                c, hf = divmod(g, 2)
                dve.wait_ge(sem("yout_mm"), g + 1)
                v.tensor_copy(yout[:, c, hf * HALF:(hf + 1) * HALF], bank[4 + g % 2][:, :]).then_inc(sem("yout_done"), 1)

        @block.gpsimd
        def _(pool):
            ind = nc.gpsimd.indirect_dma_start

            def at_rows(ap):
                return bass.IndirectOffsetOnAxis(ap=ap.bitcast(U32), axis=0)

            def moe(l):
                S_, B_ = sem, lambda name: l * PER_LAYER[name]
                for c in range(TC):
                    for v_ in range(2):
                        pool.wait_ge(S_(f"htok_set{v_}_"), B_(f"htok_set{v_}_") + c + 1)
                    pool.dma_start(hD[c * P:(c + 1) * P, :], hTok[:, c, :]).then_inc(S_("h_rows"), 16)
                pool.wait_ge(S_("slots_set"), B_("slots_set") + 1)
                pool.wait_ge(sem("tab_clear"), 16 * DEPTH)
                for n in range(TC * 2):
                    ind(out=tabD[l], out_offset=at_rows(idx[:, n:n + 1]), in_=pay[:, n // 2, n % 2, :], in_offset=None,
                        bounds_check=NWIN * P * PAIRS - 1, oob_is_err=False).then_inc(S_("tab_fill"), 16)
                pool.wait_ge(S_("tab_fill"), B_("tab_fill") + 16 * TC * 2)
                pool.dma_start(tab.rearrange("p (w q) -> p w q", w=NWIN),
                               tabD[l].rearrange("(w p q) c -> p w (q c)", w=NWIN, p=P)).then_inc(S_("tab_in"), 16)
                pool.wait_ge(S_("tab_in"), B_("tab_in") + 16)
                pool.wait_ge(S_("h_rows"), B_("h_rows") + 16 * TC)
                pool.wait_ge(S_("g_clear"), B_("g_clear") + 2)
                pool.wait_ge(S_("cum_set"), B_("cum_set") + 1)

                def slots(dst, off, done):
                    nc.gpsimd.tensor_copy(dst, tab[:, bass.ds(off, 4)]).then_inc(done, 1)

                def gather(dst, ix, done):
                    apart(pool)
                    ind(out=dst, out_offset=None, in_=hD, in_offset=at_rows(ix), bounds_check=T - 1,
                        oob_is_err=False).then_inc(done, 16)

                def scatter(src, ix, done):
                    apart(pool)
                    ind(out=yD, out_offset=at_rows(ix), in_=src, in_offset=None, bounds_check=2 * T - 1,
                        oob_is_err=False).then_inc(done, 16)

                def extra(q):
                    lo = pool.value_load(cumx[0:1, bass.ds(q, 1)], min_val=0, max_val=2 * PAIRS)
                    hi = pool.value_load(cumx[0:1, bass.ds(q + 1, 1)], min_val=0, max_val=2 * PAIRS)
                    with pool.If(hi > lo):
                        with pool.Fori(lo, hi) as x:
                            at_ = nc.s_assert_within(((x - lo + 1) * PAIRS + q) * 4, 0, NWIN * PAIRS * 4 - 4,
                                                     skip_runtime_bounds_check_because="a count is at most 384, so a window is at most 5")
                            slots(curx[:, :], at_, S_("xslots"))
                            nc.gpsimd.nop().then_inc(S_("xy_free"), 1)
                            pool.wait_ge(S_("xslots"), x + 1)
                            gather(Gx, curx[:, 0:1], S_("xgather"))
                            pool.wait_ge(S_("xy_set"), 2 * (x + 1))
                            scatter(Yx, curx[:, 1:2], S_("xscatter"))
                            pool.wait_ge(S_("xscatter"), 16 * (x + 1))

                def fetch(q, s):
                    slots(cur[:, s, :], q * 4, S_("slots"))
                    pool.wait_ge(S_("slots"), B_("slots") + q + 1)
                    gather(G[:, s, :], cur[:, s, 0:1], S_(f"gather{s}_"))

                def pair(q, s, final):
                    extra(q)
                    if not final:
                        pool.wait_ge(S_("turn_mm"), B_("turn_mm") + q + 1)
                        fetch(q + 1, 1 - s)
                    pool.wait_ge(S_("y_set"), B_("y_set") + 2 * q + 4)
                    scatter(Y[:, s, :], cur[:, s, 1:2], S_("scatter"))
                    pool.wait_ge(S_("scatter"), B_("scatter") + 16 * (q + 1))
                    nc.gpsimd.nop().then_inc(S_("y_free"), 1)

                nc.gpsimd.nop().then_inc(S_("y_free"), 2)
                fetch(0, 0)
                with pool.Fori(0, PAIRS // 2 - 1) as i:
                    for s in range(2):
                        pair(2 * i + s, s, False)
                for s in range(2):
                    pair(PAIRS - 2 + s, s, s == 1)
                nc.gpsimd.nop().then_inc(S_("rows_done"), 1)

            moe(0)
            moe(1)


_INS = ['x_prompt', 'x_sample', 'cache_k', 'cache_v', 'c', 'c_ctx', 'w_ada', 'b_ada', 'norm_mix', 'norm_ffn',
        'attn_w_q', 'attn_w_kv', 'attn_q_norm', 'attn_k_norm', 'attn_w_o', 'hy_w_in', 'hy_b_in', 'hy_short_w',
        'hy_short_b', 'hy_filt_w1', 'hy_filt_b1', 'hy_filt_w2', 'hy_filt_b2', 'hy_filt_w3', 'hy_filt_b3',
        'hy_filt_freq', 'hy_log_decay', 'hy_skip', 'hy_w_out', 'hy_b_out', 'router_group_w', 'router_group_b',
        'router_expert_w', 'router_expert_b', 'moe_w_gate', 'moe_w_up', 'moe_w_down', 'final_norm']
_OUTS = [(1, SEQ, D), (1, DEC, D), (1, 1, NKV, SEQ, HD), (1, 1, NKV, SEQ, HD)]


def kernel(**inputs):
    import concourse.bacc as _bacc
    from concourse.bass_utils import run_bass_kernel_spmd as _run

    nc = _bacc.Bacc("TRN2", target_bir_lowering=False, num_devices=1)
    given = {n: np.ascontiguousarray(inputs[n]) for n in _INS}
    given["const"] = CONST
    given["token_rows"] = token_rows()
    arrays, args = {}, {}
    for name, x in given.items():
        arrays[f"in_{name}"] = x
        args[name] = nc.dram_tensor(f"in_{name}", x.shape, mybir.dt.from_np(x.dtype), kind="ExternalInput").ap()
    for i, shape in enumerate(_OUTS):
        args[f"out_{i}"] = nc.dram_tensor(f"out_{i}_dram", shape, F32, kind="ExternalOutput").ap()
    build(nc, args)
    r = _run(nc, [arrays], core_ids=[0])
    return tuple(r.results[0][f"out_{i}_dram"] for i in range(len(_OUTS)))
```

```python
import numpy as np
import concourse.bass as bass
from concourse import mybir
from contextlib import ExitStack

F32 = mybir.dt.float32
I32 = mybir.dt.int32
U32 = mybir.dt.uint32
ALU = mybir.AluOpType
ACT = mybir.ActivationFunctionType
AX = mybir.AxisListType

P = 128
D = 1024
KD = D // P
SEQ, DEC = 128, 256
T = SEQ + DEC
TC = T // P
GRID_W = 64
DEPTH = 2
HD = 64
NH, NKV = 16, 4
NG, EG = 4, 8
NE = NG * EG
EH = D // 4
PAIRS = NE // 2
WIN = 64
NWIN = T // WIN
BANDS = 8
FEAT = 1 + 2 * BANDS
FH = 64
EPS = 1e-6
NONE = 100000
HALF = 512
NORM_CH = 2
SPANS = ((0, SEQ), (SEQ, T))

R_BADA, R_NMIX, R_NFFN, R_FIN, R_BIN = 0, 96, 112, 128, 136
R_SW, R_SB, R_SKIP, R_BOUT, R_C, R_CCTX, R_QN, R_KN = 160, 232, 256, 272, 280, 288, 296, 297
R_END = 298

PER_LAYER = dict(
    logit_mm=1, htok_mm=6, htok_set=6, mask_set=1, place_mm=1, cum_set=1, tab_in=16, lg_set=1, onehot=TC,
    sort_mm=2 * KD, sorted_act=KD, sorted_dve=KD + 1, iota_in=16,
    dn_mm=PAIRS + 1, gu_mm=PAIRS, act_set=PAIRS + 1,
    at_mm=PAIRS, at_set=PAIRS, y_set=2 * PAIRS + 4, gt_set=2 * PAIRS, silu=PAIRS,
    y_free=PAIRS + 2, ysum=KD, res_mm=KD, moe_add=2 * KD, gsub_set=1, gexp=2, dv_set=1, slots_set=1,
    tab_fill=32 * TC, slots=PAIRS, scatter=16 * PAIRS, rows_done=1, y2_in0_=32, y2_in1_=32,
    gu_in=16 * PAIRS, dn_in=8 * PAIRS)


def constants():
    cols = {}
    p = np.arange(P)
    cols["ident"] = np.eye(P)
    cols["ones"] = np.ones((P, P))
    cols["headones"] = (p[:, None] // HD == p[None, :] // HD) * 1.0
    rot = np.zeros((P, P))
    for d in range(P):
        if d % 32 < 16:
            rot[d + 16, d] = -1.0
        else:
            rot[d - 16, d] = 1.0
    cols["rot"] = rot
    t = np.arange(DEC)
    d = p % HD
    ax = HD // 2
    inv = (10000.0 ** (-np.arange(0, ax, 2, dtype=np.float32) / ax)).astype(np.float32)
    pos = np.where(d[:, None] < ax, (t // GRID_W)[None, :], (t % GRID_W)[None, :]).astype(np.float32)
    ang = pos * inv[d % 16][:, None]
    cols["cos"], cols["sin"] = np.cos(ang), np.sin(ang)
    for L in (SEQ, DEC):
        n = 2 * L
        tt, f = np.arange(L), np.arange(L)
        w = 2 * np.pi * ((tt[:, None] * f[None, :]) % n) / n
        alt = (-1.0) ** tt
        re, im = np.cos(w), -np.sin(w)
        im0 = im.copy()
        im0[:, 0] = 0.0
        imz = im0.copy()
        imz[:, 0] = alt
        fold = lambda m: m.reshape(L // P, P, -1).transpose(1, 0, 2).reshape(P, -1)
        cols[f"fwd{L}"] = fold(np.concatenate([re, imz], 1))
        cols[f"alt{L}"] = fold(2 * alt[:, None])
        wt = np.where(f == 0, 1.0, 2.0)[:, None] / n
        inv_re, inv_im = wt * re.T, wt * im0.T
        inv_im[0] = alt / n
        both = np.concatenate([inv_re, inv_im], 0)
        cols[f"inv{L}"] = both.reshape(2 * L // P, P, L).transpose(1, 0, 2).reshape(P, -1)
    feats, tneg = [], []
    for L in (SEQ, DEC):
        tn = np.linspace(0.0, 1.0, L, dtype=np.float32)
        bands = np.linspace(1e-4, BANDS - 1, BANDS, dtype=np.float32)[None, :]
        w = np.float32(2.0 * np.pi) * np.arange(L, dtype=np.float32)[:, None] / np.float32(L)
        a = (bands * w).astype(np.float64)
        feats.append(np.concatenate([tn[:, None], np.cos(a), -np.sin(a)], 1).T)
        tneg.append(-tn.reshape(-1, P).T)
    ft = np.zeros((P, T))
    ft[:FEAT] = np.concatenate(feats, 1)
    cols["feats"] = ft
    cols["tneg"] = np.concatenate(tneg, 1)
    cols["before"] = (p[:, None] < p[None, :]) * 1.0
    cols["prio"] = np.tile(np.concatenate([np.arange(NG, 0, -1), np.arange(EG, 0, -1)]), (P, 1)) * 1.0
    e = np.arange(NE)
    cols["rowbase"] = np.tile((e % 2) * (WIN * PAIRS) + e // 2, (P, 1)) * 1.0
    cols["iota"] = np.tile(np.arange(2 * T), (P, 1))
    last = ("cos", "sin", "feats", "iota")
    at, parts, where = 0, [], {}
    for name in [n for n in cols if n not in last] + list(last):
        where[name] = (at, at + cols[name].shape[1])
        at += cols[name].shape[1]
        parts.append(np.asarray(cols[name], np.float32))
    return np.concatenate(parts, 1), where


CONST, WHERE = constants()
KEPT = WHERE["cos"][0]


def token_rows():
    a = np.zeros((P, 2, TC, 4), np.int32)
    tok = np.arange(P)[:, None] + P * np.arange(TC)[None, :]
    for k in range(2):
        a[:, k, :, 0] = tok + k * T
    return a.reshape(P, TC * 8)


def build(nc, a):
    ctx = ExitStack()
    with ctx:
        def sb(name, shape, dt=F32):
            return ctx.enter_context(nc.sbuf_tensor(name, shape, dt))

        sems = {}

        def sem(name):
            if name not in sems:
                sems[name] = ctx.enter_context(nc.semaphore(name))
            return sems[name]

        yD = nc.dram_tensor("expert_rows", [2 * T, D], F32, kind="Internal").ap()
        tabD = [nc.dram_tensor(f"slot_table{l}", [NWIN * P * PAIRS, 4], I32, kind="Internal").ap()
                for l in range(DEPTH)]
        cfD = [nc.dram_tensor(f"filter_spectra{o}", [P, 6, D], F32, kind="Internal").ap() for o in range(2)]

        const = sb("const", [P, KEPT])
        C = {n: const[:, lo:hi] for n, (lo, hi) in WHERE.items() if hi <= KEPT}
        ident, ones = C["ident"], C["ones"]
        xT = sb("xT", [P, KD, T])
        hT = sb("hT", [P, KD, T])
        pc = sb("pc", [P, R_END])
        condS = sb("condS", [P, KD, 32])
        ada = sb("ada", [P, DEPTH, 6, KD, 2])
        amul = sb("amul", [P, DEPTH, 2, KD, 2])
        gbo = sb("gbo", [P, KD, 2])
        rstd = sb("rstd", [P, T])
        sq = sb("sq", [P, 2, T])
        rout = sb("rout", [P, DEPTH, KD, NG + NE])
        rbias = sb("rbias", [P, DEPTH, NG + NE])
        trow = sb("trow", [P, TC * 8], I32)
        cumx = sb("cumx", [1, PAIRS + 1], I32)
        woff = sb("woff", [1, NWIN * NE], I32)
        fcol = sb("fcol", [FH, 4])
        ring = sb("ring", [P, 24576])
        WORK = 15360
        work = sb("work", [P, WORK])

        def ws(lo, n):
            assert lo + n <= WORK, (lo, n)
            return work[:, lo:lo + n]

        bank = [ctx.enter_context(nc.psum_tensor(f"bank{i}", [P, HALF], F32)) for i in range(8)]

        xtok = ws(0, TC * D).rearrange("p (c d) -> p c d", c=TC)
        prow = ws(3072, 3 * P).rearrange("p (c d) -> p c d", c=3)
        none_tile = ws(3456, NWIN * PAIRS * 4).bitcast(I32)
        w3a = ws(0, 4096)
        eld = ws(4096, 2048).rearrange("p (b d c) -> p b d c", b=2, d=2)
        hfb = ws(6144, 3072).rearrange("p (d t c) -> p d t c", d=2, t=3)
        dec = ws(9216, 1024).rearrange("p (b c) -> p b c", b=2)
        absb = ws(10240, 1024).rearrange("p (b c) -> p b c", b=2)
        smdf = ws(11264, 3072).rearrange("p (d t c) -> p d t c", d=2, t=3)
        rn = ws(14336, 1024).rearrange("p (b c) -> p b c", b=2)
        hd1 = sb("hd1", [P, 2, T])
        w1 = hd1[0:FEAT, 1, 0:FH]
        w2 = ws(7680, FH)[0:FH, :]
        cfb = hT[:, :, :].rearrange("p k t -> p (k t)")[:, 0:3072].rearrange("p (b c) -> p b c", b=6)
        hdr = ws(6144, 2 * T).rearrange("p (b t) -> p b t", b=2)
        hdt = ws(6144 + 2 * T, T)
        C["feats"] = ws(6144 + 3 * T, T)
        eps_col = sb("eps_col", [P, 1])
        PI_F = float(np.float32(3.1415925))
        adaR = sq[:, :, 0:256]
        qT = ws(0, 3072).rearrange("p (c t) -> p c t", c=KD)
        kT = ws(3072, 1024).rearrange("p (c t) -> p c t", c=2)
        V = ws(4096, 1024).rearrange("p (c d) -> p c d", c=4)
        oT = ws(5120, 3072).rearrange("p (c t) -> p c t", c=KD)
        prob = ws(8192, 4 * 896).rearrange("p (b c) -> p b c", b=4)
        probT = ws(11776, 4 * 896).rearrange("p (b c) -> p b c", b=4)
        raw = ws(11776, 2 * T).rearrange("p (b c) -> p b c", b=2)
        rq = ws(12544, 2 * T).rearrange("p (b c) -> p b c", b=2)
        rs_ = ws(13312, 2 * DEC).rearrange("p (b c) -> p b c", b=2)
        ck = ws(13824, 256)
        ktok = ws(14080, 256)
        C["cos"], C["sin"] = ws(14336, DEC), ws(14336 + DEC, DEC)
        sm = ws(13568, 1408)
        tab = ws(14976, NWIN * PAIRS * 4).bitcast(I32)
        hTok = ws(0, TC * D).rearrange("p (c d) -> p c d", c=TC)
        onehot = ws(3072, TC * 2 * T).rearrange("p (c s) -> p c s", c=TC)
        iota = ws(5376, 2 * T)
        SORTED = 2 * T + WIN
        hS = ws(6144, KD * SORTED).rearrange("p (k s) -> p k s", k=KD)
        Y = ws(0, 2 * D).rearrange("p (b d) -> p b d", b=2)
        Yx = ws(2048, D)
        GT = ws(3072, D).rearrange("p (k s) -> p k s", k=KD)
        GTx = ws(4096, D).rearrange("p (k s) -> p k s", k=KD)
        S = ws(12800, EH)
        A = ws(13056, EH)
        AT = ws(13312, EH).rearrange("p (k s) -> p k s", k=2)
        cur = sb("cur", [P, 2, 4], I32)
        curx = sb("curx", [P, 4], I32)
        y2 = ws(0, 2 * TC * D).rearrange("p (k c d) -> p k c d", k=2, c=TC)
        UW = T + 1
        st = ws(0, 3 * KD * UW).rearrange("p (s k t) -> p s k t", s=3, k=KD)
        upad = ws(3 * KD * UW, 2 * (UW + 2)).rearrange("p (b c) -> p b c", b=2)
        cv = ws(3 * KD * UW + 2 * (UW + 2), 2 * UW).rearrange("p (b c) -> p b c", b=2)
        HX = 3 * KD * UW + 4 * UW + 4
        ztok = hT[:, :, :].rearrange("p k t -> p (k t)").rearrange("p (c d) -> p c d", c=TC)
        prod = ws(HX, 4 * HALF).rearrange("p (b c) -> p b c", b=4)
        ztmp = ws(HX + 4 * HALF, T)
        ytmp = ws(HX + 4 * HALF + T, T)
        Yf = ring[:, 0:6 * D].rearrange("p (f c) -> p f c", f=6)
        cf = ring[:, 6 * D:12 * D].rearrange("p (f c) -> p f c", f=6)
        wout = ring[:, 12 * D:20 * D].rearrange("p (k n) -> p k n", k=KD)
        yout = ws(0, TC * D).rearrange("p (c d) -> p c d", c=TC)

        def conv_cols(lo, hi):
            return (lo, hi) if hi <= SEQ else (lo + 1, hi + 1)

        def ada_tile(n):
            return ring[:, (n % 3) * 8192:(n % 3 + 1) * 8192].rearrange("p (k n) -> p k n", k=KD)

        wq = ring[:, 0:8192].rearrange("p (k n) -> p k n", k=KD)
        wkv = ring[:, 8192:12288].rearrange("p (k n) -> p k n", k=KD)
        wo = ring[:, 12288:20480].rearrange("p (c n) -> p c n", c=KD)
        win = [ring[:, 4096 * i:4096 * (i + 1)].rearrange("p (k n) -> p k n", k=KD) for i in range(6)]
        WIN_GROUP = [0, 0, 1, 2, 2, 3]
        WIN_ORDER = [4, 5, 0, 1, 2, 3]

        def slot_gu(s):
            return ring[:, s * 12288:s * 12288 + 8192].rearrange("p (u j k h) -> p u j k h", u=2, j=2, k=KD)

        def slot_dn(s):
            return ring[:, s * 12288 + 8192:(s + 1) * 12288].rearrange("p (j k n) -> p j k n", j=2, k=2)

        at = [0]

        def small(*shape):
            n = int(np.prod(shape))
            v = sm[:, at[0]:at[0] + n]
            at[0] += n
            assert at[0] <= 1408
            if len(shape) == 2:
                return v.rearrange("p (a b) -> p a b", a=shape[0])
            if len(shape) == 3:
                return v.rearrange("p (a b c) -> p a b c", a=shape[0], b=shape[1])
            return v

        lg = small(TC, NG + NE)
        gmax, gden, v1, v2, ev, den, w1r, w2r = [small(TC, 1) for _ in range(8)]
        gx, geq, goh = [small(TC, NG) for _ in range(3)]
        esel, eeq, oh1, oh2, e2 = [small(TC, EG) for _ in range(5)]
        etmp = small(TC, EG)
        masks = small(2, TC, NE)
        m_all = small(TC, NE)
        mtmp = [small(2, TC, NE) for _ in range(3)]
        posk, rowk, wck, basek, startk, spos, wink = [small(2, TC) for _ in range(7)]
        start = small(2, 64)
        idx = sb("idx", [P, TC * 2], I32)
        pay = sb("pay", [P, 2, TC, 4], I32)
        cnt = ws(12800, 320)[0:1]
        mx = sb("mx", [P, 2, 3])
        nb = sb("nb", [P, 2, 3])
        rsum = sb("rsum", [P, 2, 3])
        rinv = sb("rinv", [P, 2, 3])

        NADA = DEPTH * 6
        FILT = [(o, n) for o in range(2) for n in range(2)]
        FILT_AFTER = {1: 0, 3: 1, 5: 2, 7: 3}
        QK = 10

        def chunk_dst(m, lo, hi):
            return kT[:, m, lo:hi] if m < 2 else qT[:, m - 2, lo:hi]

        x_in = [a["x_prompt"][0], a["x_sample"][0, 0:P], a["x_sample"][0, P:2 * P]]
        y_out = [a["out_0"][0], a["out_1"][0, 0:P], a["out_1"][0, P:2 * P]]
        rows = lambda v, n: v.rearrange("(r c) -> r c", c=P)
        param_rows = [
            (R_BADA, a["b_ada"].rearrange("l (r c) -> (l r) c", c=P)),
            (R_NMIX, a["norm_mix"].rearrange("l (r c) -> (l r) c", c=P)),
            (R_NFFN, a["norm_ffn"].rearrange("l (r c) -> (l r) c", c=P)),
            (R_FIN, rows(a["final_norm"], 8)),
            (R_BIN, rows(a["hy_b_in"][0], 24)),
            (R_SW, a["hy_short_w"][0].rearrange("w (r c) -> (w r) c", c=P)),
            (R_SB, rows(a["hy_short_b"][0], 24)),
            (R_SKIP, a["hy_skip"][0].rearrange("w (r c) -> (w r) c", c=P)),
            (R_BOUT, rows(a["hy_b_out"][0], 8)),
            (R_C, rows(a["c"][0], 8)),
            (R_CCTX, rows(a["c_ctx"], 8)),
        ]

        def prow_at(r, n):
            assert r // P == (r + n - 1) // P
            return prow[r % P:r % P + n, r // P, :]

        block = ctx.enter_context(nc.Block())

        def load_ada(sp, t):
            if t >= 3:
                sp.wait_ge(sem("ada_mm"), t - 2)
            l, s = divmod(t, 6)
            sp.dma_start(ada_tile(t), a["w_ada"][l, :, s * D:(s + 1) * D].rearrange("(k p) n -> p k n", p=P))\
                .then_inc(sem(f"ada_in{t % 3}"), 16)

        def load_decay(sp, f):
            if f >= 2:
                sp.wait_ge(sem("dec_set"), 6 * (f - 1))
            o, n = FILT[f]
            for d in range(2):
                lo = (2 * o + d) * D + n * HALF
                sp.dma_start(eld[:, f % 2, d, :], a["hy_log_decay"][0, lo:lo + HALF].partition_broadcast(P))\
                    .then_inc(sem(f"decay_in{f % 2}"), 16)

        def load_pair(sp, l, s, q, behind=False):
            gu, dn = slot_gu(s), slot_dn(s)
            for u, name in enumerate(("moe_w_gate", "moe_w_up")):
                sp.dma_start(gu[:, u].rearrange("p j k h -> p j (k h)"),
                             a[name][l, bass.ds(2 * q, 2)].rearrange("j (p k) h -> p j (k h)", p=P))\
                    .then_inc(sem(f"gu_in_{s}"), 16)
            if behind:
                sp.wait_ge(sem("dn_mm"), l * PER_LAYER["dn_mm"] + q - 1 + 1)
            sp.dma_start(dn, a["moe_w_down"][l, bass.ds(2 * q, 2)].rearrange("j (k p) n -> p j k n", p=P))\
                .then_inc(sem(f"dn_in_{s}"), 16)

        def moe_loads(sp, l):
            with sp.Fori(1, PAIRS // 2) as i:
                for s in range(2):
                    sp.wait_ge(sem("gu_mm"), l * PER_LAYER["gu_mm"] + 2 * i + s - 1)
                    load_pair(sp, l, s, 2 * i + s, behind=True)
            sp.wait_ge(sem("rows_done"), l * PER_LAYER["rows_done"] + 1)
            for hf in range(2):
                for k in range(2):
                    cols = slice(hf * HALF, (hf + 1) * HALF)
                    sp.dma_start(y2[:, k, :, cols], yD[k * T:(k + 1) * T, cols].rearrange("(c p) d -> p c d", p=P))\
                        .then_inc(sem(f"y2_in{hf}_"), 16)

        def load_iota(sp):
            sp.wait_ge(sem("kv_out"), 32)
            sp.dma_start(iota, a["const"][:, WHERE["iota"][0]:WHERE["iota"][1]]).then_inc(sem("iota_in"), 16)

        def load_win(sp, n):
            c = WIN_ORDER[n]
            sp.dma_start(win[n], a["hy_w_in"][0, :, c * HALF:(c + 1) * HALF].rearrange("(k p) n -> p k n", p=P))\
                .then_inc(sem(f"win_in{WIN_GROUP[n]}"), 16)

        def further(at, top):
            return nc.s_assert_within(at, 0, top,
                                      skip_runtime_bounds_check_because="a count is at most 384, so a window is at most 5")

        def apart(eng):
            eng.sem_inc(sem("passed"), 1)

        @block.sync
        def _(sp):
            for r0, src in param_rows:
                sp.dma_start(prow_at(r0, src.shape[0]), src).then_inc(sem("tables_in"), 16)
            for r0, name in ((R_QN, "attn_q_norm"), (R_KN, "attn_k_norm")):
                for b in range(2):
                    sp.dma_start(prow[r0 % P:r0 % P + 1, 2, b * HD:(b + 1) * HD], a[name])\
                        .then_inc(sem("tables_in"), 16)
            sp.dma_start(const[:, :], a["const"][:, 0:KEPT]).then_inc(sem("tables_in"), 16)
            for c in range(TC):
                sp.dma_start(xtok[:, c, :], x_in[c]).then_inc(sem("x_in"), 16)
            sp.dma_start(w1, a["hy_filt_w1"][0]).then_inc(sem("filt_small_in"), 16)
            sp.dma_start(C["feats"], a["const"][:, WHERE["feats"][0]:WHERE["feats"][1]]).then_inc(sem("filt_small_in"), 16)
            sp.dma_start(w2[:, :], a["hy_filt_w2"][0]).then_inc(sem("filt_small_in"), 16)
            for i, name in enumerate(("hy_filt_b1", "hy_filt_b2", "hy_filt_freq")):
                sp.dma_start(fcol[:, i:i + 1], a[name][0].rearrange("(p a) -> p a", a=1))\
                    .then_inc(sem("filt_small_in"), 16)
            load_ada(sp, 0)
            sp.wait_ge(sem("preset"), 3)
            for l in range(DEPTH):
                sp.dma_start(tabD[l].rearrange("(w p q) c -> p w (q c)", w=NWIN, p=P),
                             none_tile.rearrange("p (w q) -> p w q", w=NWIN)).then_inc(sem("tab_clear"), 16)
            sp.wait_ge(sem("xT_done"), KD)
            sp.wait_ge(sem("pc_done"), 1)
            sp.wait_ge(sem("tab_clear"), 16 * DEPTH)
            sp.dma_start(w3a[0:FH, :], a["hy_filt_w3"][0]).then_inc(sem("w3_in"), 16)
            sp.dma_start(w3a[FH:FH + 1, :], a["hy_filt_b3"]).then_inc(sem("w3_in"), 16)
            load_decay(sp, 0)
            for t in range(1, 3):
                load_ada(sp, t)
            sp.dma_start(trow[:, :], a["token_rows"]).then_inc(sem("rout_in"), 16)
            for l in range(DEPTH):
                sp.dma_start(rout[:, l, :, 0:NG], a["router_group_w"][l].rearrange("(k p) g -> p k g", p=P))\
                    .then_inc(sem("rout_in"), 16)
                sp.dma_start(rout[:, l, :, NG:], a["router_expert_w"][l].rearrange("(k p) g e -> p k (g e)", p=P))\
                    .then_inc(sem("rout_in"), 16)
                sp.dma_start(rbias[:, l, 0:NG], a["router_group_b"][l].partition_broadcast(P))\
                    .then_inc(sem("rout_in"), 16)
                sp.dma_start(rbias[:, l, NG:], a["router_expert_b"][l].rearrange("g e -> (g e)").partition_broadcast(P))\
                    .then_inc(sem("rout_in"), 16)
            for t in range(3, NADA):
                load_ada(sp, t)
                if t - 3 in FILT_AFTER and FILT_AFTER[t - 3] + 1 < 4:
                    load_decay(sp, FILT_AFTER[t - 3] + 1)
            sp.wait_ge(sem("ada_mm"), NADA)
            sp.dma_start(wkv, a["attn_w_kv"][0].rearrange("(k p) n -> p k n", p=P)).then_inc(sem("wkv_in"), 16)
            sp.dma_start(wq, a["attn_w_q"][0].rearrange("(k p) n -> p k n", p=P)).then_inc(sem("wq_in"), 16)
            wo_v = a["attn_w_o"][0].rearrange("(g b m d) n -> b d g m n", g=2, b=2, m=4)
            for b in range(2):
                for g in range(2):
                    sp.dma_start(wo[b * HD:(b + 1) * HD, 4 * g:4 * g + 4, :], wo_v[b, :, g]).then_inc(sem("wo_in"), 16)
            sp.wait_ge(sem("cf_out"), 16 * 24)
            sp.dma_start(ck.rearrange("p (h d) -> p h d", h=NKV), a["cache_k"][0, 0].rearrange("h s d -> s h d"))\
                .then_inc(sem("cache_in"), 16)
            sp.dma_start(V[:, 3, :].rearrange("p (h d) -> p h d", h=NKV), a["cache_v"][0, 0].rearrange("h s d -> s h d"))\
                .then_inc(sem("cache_in"), 16)
            sp.dma_start(work[:, 14336:14336 + 2 * DEC], a["const"][:, WHERE["cos"][0]:WHERE["sin"][1]])\
                .then_inc(sem("cache_in"), 16)
            sp.wait_ge(sem("v_done"), TC)
            sp.dma_start(a["out_3"][0, 0].rearrange("h s d -> s h d"), V[:, 0, :].rearrange("p (h d) -> p h d", h=NKV))\
                .then_inc(sem("kv_out"), 16)
            sp.wait_ge(sem("ktok_done"), 1)
            sp.dma_start(a["out_2"][0, 0].rearrange("h s d -> s h d"), ktok.rearrange("p (h d) -> p h d", h=NKV))\
                .then_inc(sem("kv_out"), 16)
            sp.wait_ge(sem("qk_mm"), QK)
            sp.wait_ge(sem("v_mm"), TC)
            load_pair(sp, 0, 0, 0)
            sp.wait_ge(sem("mix0_mm"), KD)
            load_iota(sp)
            load_pair(sp, 0, 1, 1)
            moe_loads(sp, 0)
            sp.wait_ge(sem("gu_mm"), PAIRS - 1)
            for n in (0, 1):
                load_win(sp, n)
            sp.wait_ge(sem("dn_mm"), PAIRS - 1 + 1)
            load_win(sp, 2)
            sp.wait_ge(sem("gu_mm"), PAIRS)
            for n in (3, 4):
                load_win(sp, n)
            sp.wait_ge(sem("dn_mm"), PAIRS + 1)
            load_win(sp, 5)
            sp.wait_ge(sem("hin_mm"), 24)
            sp.wait_ge(sem("cf_out"), 16 * 24)
            sp.dma_start(cf, cfD[0]).then_inc(sem("cf_in0"), 16)
            sp.dma_start(wout, a["hy_w_out"][0].rearrange("(k p) n -> p k n", p=P)).then_inc(sem("wout_in"), 16)
            sp.wait_ge(sem("cprod"), 6)
            sp.dma_start(cf, cfD[1]).then_inc(sem("cf_in1"), 16)
            sp.wait_ge(sem("cprod"), 12)
            sp.wait_ge(sem("inv_mm"), 2 * KD)
            load_pair(sp, 1, 0, 0)
            sp.wait_ge(sem("mix1_mm"), KD)
            load_iota(sp)
            load_pair(sp, 1, 1, 1)
            moe_loads(sp, 1)
            for c in range(TC):
                sp.wait_ge(sem("yout_done"), 2 * (c + 1))
                sp.dma_start(y_out[c], yout[:, c, :]).then_inc(sem("y_out"), 16)
            sp.wait_ge(sem("y_out"), 16 * TC)
            sp.wait_ge(sem("kv_out"), 32)

        @block.tensor
        def _(pe):
            mm = nc.tensor.matmul
            tr = nc.tensor.transpose

            pe.wait_ge(sem("tables_in"), 16 * (len(param_rows) + 5))
            for i, n in enumerate((P, P, R_END - 2 * P)):
                last = tr(bank[7][:, i * P:i * P + n], prow[0:n, i, :], ident[0:n, 0:n])
            last.then_inc(sem("pc_mm"), 1)
            pe.wait_ge(sem("x_in"), 16 * TC)
            for k in range(KD):
                if k >= 4:
                    pe.wait_ge(sem("xT_done"), k - 3)
                for c in range(TC):
                    last = tr(bank[k % 4][:, c * P:(c + 1) * P], xtok[:, c, k * P:(k + 1) * P], ident)
                last.then_inc(sem("xT_mm"), 1)

            pe.wait_ge(sem("filt_small_in"), 16 * 6)
            mm(bank[4][0:FH, 0:T], w1, C["feats"][0:FEAT, :], start=True, stop=True).then_inc(sem("mlp_mm"), 1)
            pe.wait_ge(sem("mlp_done"), 1)
            mm(bank[5][0:FH, 0:T], w2[:, :], hd1[0:FH, 0, :], start=True, stop=True).then_inc(sem("mlp_mm"), 1)

            def ada_mm(t):
                pe.wait_ge(sem(f"ada_in{t % 3}"), 16 * (t // 3 + 1))
                if t >= 2:
                    pe.wait_ge(sem("adaR_set"), t - 1)
                w = ada_tile(t)
                for k in range(KD):
                    for j in range(4):
                        last = mm(bank[t % 2][32 * j:32 * j + 32, 0:256], condS[:, k, :],
                                  w[:, k, 256 * j:256 * j + 256], start=(k == 0), stop=(k == KD - 1))
                last.then_inc(sem("ada_mm"), 1)

            def ada_tr(t):
                pe.wait_ge(sem("adaR_set"), t + 1)
                if t >= 1:
                    pe.wait_ge(sem("ada_done"), t)
                for u in range(2):
                    last = tr(bank[2][:, u * P:(u + 1) * P], adaR[:, t % 2, u * P:(u + 1) * P], ident)
                last.then_inc(sem("ada_tr"), 1)

            def taps(f):
                o, n = FILT[f]
                if f == 0:
                    pe.wait_ge(sem("mlp_done"), 2)
                    pe.wait_ge(sem("w3_in"), 32)
                if f >= 1:
                    pe.wait_ge(sem("rn_set"), 2 * f)
                    pe.wait_ge(sem("cf_set"), 6 * f)
                for i, (d, c) in enumerate((d, c) for d in range(2) for c in range(3)):
                    g = 6 * f + i
                    if g >= 2:
                        pe.wait_ge(sem("taps_done"), g - 1)
                    lo = (2 * o + d) * D + n * HALF
                    mm(bank[4 + g % 2][:, :], hd1[0:FH + 1, 1, c * P:(c + 1) * P], w3a[0:FH + 1, lo:lo + HALF],
                       start=True, stop=True).then_inc(sem("taps_mm"), 1)
                    if i >= 1:
                        size_sum(f, i - 1)
                size_sum(f, 5)

            def spectra(f):
                pe.wait_ge(sem("smdf_done"), 6 * (f + 1))
                for i in range(6):
                    g = 6 * f + i
                    if g >= 2:
                        pe.wait_ge(sem("cf_set"), g - 1)
                    b = bank[4 + g % 2]
                    r = i % 2
                    if i < 2:
                        ops = [(C["fwd256"], c * 512 + r * P, 0, 1 + c) for c in range(2)]
                    elif i < 4:
                        ops = [(C["fwd256"], c * 512 + 256 + r * P, 1, 1 + c) for c in range(2)]
                    elif i == 4:
                        ops = [(C["fwd128"], 0, 0, 0)]
                    else:
                        ops = [(C["fwd128"], P, 1, 0)]
                    if i == 0:
                        pe.wait_ge(sem("taps_done"), 6 * (f + 1))
                    top = {2: [(C["alt256"][:, c:c + 1], 1 + c) for c in range(2)], 5: [(C["alt128"], 0)]}.get(i, [])
                    for j, (m, off, d, c) in enumerate(ops):
                        last = mm(b[:, :], m[:, off:off + P], smdf[:, d, c, :], start=(j == 0),
                                  stop=(j == len(ops) - 1))
                    for j, (col, c) in enumerate(top):
                        last = mm(b[0:1, :], col, hfb[:, 1, c, :], start=False, stop=True, skip_group_check=True)
                    last.then_inc(sem("cf_mm"), 1)

            def size_sum(f, i):
                d, c = divmod(i, 3)
                g = 6 * f + i
                pe.wait_ge(sem("abs_done"), g + 1)
                b = bank[6] if c == 0 else bank[7]
                last = mm(b[:, :], ones, absb[:, g % 2, :], start=(d == 0 and c <= 1), stop=(d == 1 and c != 1))
                last.then_inc(sem("size_mm"), 1)

            pe.wait_ge(sem("cond_set"), 2)
            pe.wait_ge(sem("xT_done"), KD)
            pe.wait_ge(sem("pc_done"), 1)
            for t in range(NADA):
                ada_mm(t)
                if t >= 1:
                    ada_tr(t - 1)
                if t in FILT_AFTER:
                    taps(FILT_AFTER[t])
                if t - 1 in FILT_AFTER:
                    spectra(FILT_AFTER[t - 1])
            ada_tr(NADA - 1)

            def norm_sum(n, k):
                if n > 0 and k == 0:
                    pe.wait_ge(sem("rt_done"), n)
                pe.wait_ge(sem("sq_done"), KD * n + k + 1)
                mm(bank[3][:, 0:T], ones, sq[:, k % 2, :], start=(k == 0), stop=(k == KD - 1)).then_inc(sem("sq_mm"), 1)

            for k in range(KD):
                norm_sum(0, k)
            pe.wait_ge(sem("h_done"), 2 * KD)
            pe.wait_ge(sem("wkv_in"), 16)
            pe.wait_ge(sem("cf_set"), 24)

            def qk_mm(m):
                if m == 2:
                    pe.wait_ge(sem("wq_in"), 16)
                if m >= 2:
                    pe.wait_ge(sem("raw_set"), m - 1)
                for k in range(KD):
                    if m < 2:
                        last = mm(bank[m % 2][:, 0:T], wkv[:, k, m * P:(m + 1) * P], hT[:, k, :],
                                  start=(k == 0), stop=(k == KD - 1))
                    else:
                        g, mq = divmod(m - 2, 4)
                        for b in range(2):
                            h = 8 * g + 4 * b + mq
                            last = mm(bank[m % 2][b * HD:(b + 1) * HD, 0:T], wq[:, k, h * HD:(h + 1) * HD], hT[:, k, :],
                                      start=(k == 0), stop=(k == KD - 1))
                last.then_inc(sem("qk_mm"), 1)

            def qk_ss(m):
                pe.wait_ge(sem("qsq_set"), m + 1)
                if m >= 2:
                    pe.wait_ge(sem("qrt_set"), m - 1)
                mm(bank[4 + m % 2][:, 0:T], C["headones"], sq[:, m % 2, :], start=True, stop=True).then_inc(sem("qss_mm"), 1)

            def qk_rot(m):
                pe.wait_ge(sem("qn_set"), m + 1)
                if m >= 2:
                    pe.wait_ge(sem("qs_set"), m - 1)
                mm(bank[6 + m % 2][:, 0:DEC], C["rot"], chunk_dst(m, SEQ, T), start=True, stop=True).then_inc(sem("rot_mm"), 1)

            for m in range(QK + 2):
                if m < QK:
                    qk_mm(m)
                if 1 <= m <= QK:
                    qk_ss(m - 1)
                if m >= 2:
                    qk_rot(m - 2)
            pe.wait_ge(sem("raw_set"), QK)
            for c in range(TC):
                if c >= 2:
                    pe.wait_ge(sem("v_done"), c - 1)
                for k in range(KD):
                    last = mm(bank[c % 2][:, 0:256], hT[:, k, c * P:(c + 1) * P], wkv[:, k, 256:512],
                              start=(k == 0), stop=(k == KD - 1))
                last.then_inc(sem("v_mm"), 1)
            pe.wait_ge(sem("cache_in"), 48)
            pe.wait_ge(sem("qs_set"), QK)
            pe.wait_ge(sem("qrt_set"), QK)
            for c in range(2):
                last = tr(bank[6][:, c * P:(c + 1) * P], ck[:, c * P:(c + 1) * P], ident)
            last.then_inc(sem("ck_mm"), 1)
            for c in range(2):
                last = tr(bank[7][:, c * P:(c + 1) * P], kT[:, c, 0:P], ident)
            last.then_inc(sem("ktok_mm"), 1)

            def scores(c):
                g = c // 4
                if c >= 1:
                    pe.wait_ge(sem("exp_done"), 6 * c)
                halves = [slice(b * HD, (b + 1) * HD) for b in range(2)]
                for b, r in enumerate(halves):
                    mm(bank[2 * b][:, 0:T], qT[r, c, P:2 * P], kT[r, g, P:512], start=True, stop=True)
                for b, r in enumerate(halves):
                    mm(bank[2 * b + 1][:, 0:T], qT[r, c, 2 * P:3 * P], kT[r, g, P:512], start=True, stop=True)
                for b, r in enumerate(halves):
                    mm(bank[2 * b + 1][:, T:512], qT[r, c, 0:P], kT[r, g, 0:P], start=True, stop=True).then_inc(sem("score_mm"), 1)

            def prob_tr(n):
                pe.wait_ge(sem("prob_done"), 3 * (n + 1))
                if n >= 1:
                    pe.wait_ge(sem("probTa_set"), n)
                    pe.wait_ge(sem("probTb_set"), n)
                pr = prob[:, n % 4, :]
                for kc in range(3):
                    for q in range(2):
                        b, off = (bank[4], kc * 256 + q * P) if kc < 2 else (bank[5], q * P)
                        tr(b[:, off:off + P], pr[:, q * T + kc * P:q * T + (kc + 1) * P], ident)
                tr(bank[5][:, 256:T], pr[:, 768:896], ident).then_inc(sem("probT_mm"), 1)

            def values(c):
                pe.wait_ge(sem("probTa_set"), 2 * c + 2)
                pe.wait_ge(sem("probTb_set"), 2 * c + 2)
                if c >= 2:
                    pe.wait_ge(sem("oT_set"), c - 1)
                O = bank[6 + c % 2]
                heads = [(slice(b * HD, (b + 1) * HD), 2 * (c // 4) + b, probT[:, (2 * c + b) % 4, :]) for b in range(2)]
                for r, g, pt in heads:
                    mm(O[r, 0:P], V[:, 0, g * HD:(g + 1) * HD], pt[:, 768:896], start=True, stop=True)
                for kc in range(3):
                    for r, g, pt in heads:
                        last = mm(O[r, P:T], V[:, 1 + kc, g * HD:(g + 1) * HD], pt[:, kc * 256:(kc + 1) * 256],
                                  start=(kc == 0), stop=(kc == 2))
                last.then_inc(sem("oT_mm"), 2)

            pe.wait_ge(sem("v_done"), TC)
            pe.wait_ge(sem("ck_set"), 1)
            pe.wait_ge(sem("qk_done"), QK)
            pe.wait_ge(sem("ktok_done"), 1)
            for c in range(KD + 2):
                if c < KD:
                    scores(c)
                if 1 <= c <= KD:
                    prob_tr(2 * c - 2)
                if c >= 2:
                    values(c - 2)
                if 1 <= c <= KD:
                    prob_tr(2 * c - 1)
            pe.wait_ge(sem("wo_in"), 64)
            pe.wait_ge(sem("oT_set"), KD)
            for m in range(KD):
                if m >= 2:
                    pe.wait_ge(sem("mix0_done"), 2 * (m - 1))
                for k in range(KD):
                    last = mm(bank[m % 2][:, 0:T], wo[:, k, m * P:(m + 1) * P], oT[:, k, :],
                              start=(k == 0), stop=(k == KD - 1))
                last.then_inc(sem("mix0_mm"), 1)
                if m >= 2:
                    norm_sum(1, m - 2)
            for k in (KD - 2, KD - 1):
                norm_sum(1, k)

            def moe(l, n_norm):
                S_, B_ = sem, lambda name: l * PER_LAYER[name]
                pe.wait_ge(sem("h_done"), 2 * KD * (n_norm + 1))
                pe.wait_ge(sem("rout_in"), 16 * 9)
                for c in range(TC):
                    for k in range(KD):
                        last = mm(bank[0][:, c * 64:c * 64 + NG + NE], hT[:, k, c * P:(c + 1) * P], rout[:, l, k, :],
                                  start=(k == 0), stop=(k == KD - 1))
                last.then_inc(S_("logit_mm"), 1)
                for g in range(2 * TC):
                    c, hf = divmod(g, 2)
                    if g >= 2:
                        pe.wait_ge(S_("htok_set"), B_("htok_set") + g - 1)
                    for k in range(4):
                        last = tr(bank[4 + g % 2][:, k * P:(k + 1) * P], hT[:, 4 * hf + k, c * P:(c + 1) * P], ident)
                    last.then_inc(S_("htok_mm"), 1)
                pe.wait_ge(S_("mask_set"), B_("mask_set") + 1)
                for c in range(TC):
                    mm(bank[1][:, 256:256 + NE], ones, m_all[:, c], start=(c == 0), stop=(c == TC - 1))
                for c in range(TC):
                    for c2 in range(c + 1):
                        last = mm(bank[1][:, c * 64:c * 64 + NE], C["before"] if c2 == c else ones,
                                  m_all[:, c2], start=(c2 == 0), stop=(c2 == c))
                last.then_inc(S_("place_mm"), 1)
                pe.wait_ge(S_("htok_set"), B_("htok_set") + 2 * TC)
                pe.wait_ge(S_("onehot"), B_("onehot") + TC)
                for g in range(2 * KD):
                    k, hf = divmod(g, 2)
                    if g >= 4:
                        if g % 2:
                            pe.wait_ge(S_("sorted_dve"), B_("sorted_dve") + (g - 4) // 2 + 2)
                        else:
                            pe.wait_ge(S_("sorted_act"), B_("sorted_act") + (g - 4) // 2 + 1)
                    for c in range(TC):
                        last = mm(bank[4 + g % 4][:, 0:T], hTok[:, c, k * P:(k + 1) * P], onehot[:, c, hf * T:(hf + 1) * T],
                                  start=(c == 0), stop=(c == TC - 1))
                    last.then_inc(S_("sort_mm"), 1)
                pe.wait_ge(S_("cum_set"), B_("cum_set") + 1)

                def gate_up(gt, s, done):
                    gu = slot_gu(s)
                    for k in range(KD):
                        for j in range(2):
                            last = mm(bank[2][WIN * j:WIN * (j + 1), :], gt[:, k, WIN * j:WIN * (j + 1)], gu[:, :, j, k, :],
                                      start=(k == 0), stop=(k == KD - 1))
                    last.then_inc(done, 1)

                def turn_act(done):
                    for k in range(2):
                        last = tr(bank[3][:, k * P:(k + 1) * P], A[:, k * P:(k + 1) * P], ident)
                    last.then_inc(done, 1)

                def down(s, b, done):
                    dn = slot_dn(s)
                    for hf in range(2):
                        for k in range(2):
                            for j in range(2):
                                last = mm(bank[b + hf][WIN * j:WIN * (j + 1), :], AT[:, k, WIN * j:WIN * (j + 1)],
                                          dn[:, j, k, hf * HALF:(hf + 1) * HALF], start=(k == 0), stop=(k == 1))
                    last.then_inc(done, 1)

                def extra(q, s, i):
                    apart(pe)
                    lo = pe.value_load(cumx[0:1, bass.ds(q, 1)], min_val=0, max_val=2 * PAIRS)
                    hi = pe.value_load(cumx[0:1, bass.ds(q + 1, 1)], min_val=0, max_val=2 * PAIRS)
                    with pe.If(hi > lo):
                        pe.wait_ge(S_("y_set"), B_("y_set") + 2 * q + 4)
                        pe.wait_ge(sem(f"dn_in_{s}"), B_("dn_in") + 16 * (i + 1))
                        apart(pe)
                        with pe.Fori(lo, hi) as x:
                            pe.wait_ge(S_("xgt_set"), 2 * (x + 1))
                            gate_up(GTx, s, S_("xgu_mm"))
                            pe.wait_ge(S_("xact_set"), x + 1)
                            turn_act(S_("xat_mm"))
                            pe.wait_ge(S_("xat_set"), x + 1)
                            down(s, 4, S_("xdn_mm"))
                            pe.wait_ge(S_("xy_set"), 2 * (x + 1))

                def pair(q, s, i):
                    pe.wait_ge(sem(f"gu_in_{s}"), B_("gu_in") + 32 * (i + 1))
                    pe.wait_ge(S_("gt_set"), B_("gt_set") + 2 * (q + 1))
                    pe.wait_ge(S_("act_set"), B_("act_set") + q + 1)
                    extra(q, s, i)
                    gate_up(GT, s, S_("gu_mm"))
                    pe.wait_ge(S_("act_set"), B_("act_set") + q + 2)
                    turn_act(S_("at_mm"))
                    pe.wait_ge(S_("at_set"), B_("at_set") + q + 1)
                    pe.wait_ge(sem(f"dn_in_{s}"), B_("dn_in") + 16 * (i + 1))
                    pe.wait_ge(S_("y_set"), B_("y_set") + 2 * q + 2)
                    down(s, 4 + 2 * s, S_("dn_mm"))

                nc.tensor.nop().then_inc(S_("dn_mm"), 1)
                pe.wait_ge(S_("sorted_act"), B_("sorted_act") + KD)
                pe.wait_ge(S_("sorted_dve"), B_("sorted_dve") + KD + 1)
                with pe.Fori(0, PAIRS // 2) as i:
                    for s in range(2):
                        pair(2 * i + s, s, i)
                for k in range(KD):
                    if k == 0:
                        pe.wait_ge(S_("y_set"), B_("y_set") + 2 * PAIRS + 4)
                    pe.wait_ge(S_("ysum"), B_("ysum") + k + 1)
                    if k >= 2:
                        pe.wait_ge(S_("moe_add"), B_("moe_add") + 2 * (k - 1))
                    for c in range(TC):
                        last = tr(bank[k % 2][:, c * P:(c + 1) * P], y2[:, 0, c, k * P:(k + 1) * P], ident)
                    last.then_inc(S_("res_mm"), 1)
                    if k >= 2:
                        norm_sum(n_norm + 1, k - 2)
                for k in (KD - 2, KD - 1):
                    norm_sum(n_norm + 1, k)

            moe(0, 1)

            pe.wait_ge(sem("h_done"), 2 * KD * 3)
            for n in range(24):
                if n % 4 == 0:
                    g = WIN_GROUP[n // 4]
                    pe.wait_ge(sem(f"win_in{g}"), 16 * WIN_GROUP.count(g))
                if n >= 2:
                    pe.wait_ge(sem("u_set"), 2 * (n - 1))
                w = win[n // 4]
                for k in range(KD):
                    last = mm(bank[n % 2][:, 0:T], w[:, k, (n % 4) * P:(n % 4 + 1) * P], hT[:, k, :],
                              start=(k == 0), stop=(k == KD - 1))
                last.then_inc(sem("hin_mm"), 1)
            for o in range(2):
                if o == 0:
                    pe.wait_ge(sem("conv_done"), 24)
                for g in range(2 * TC):
                    c, hf = divmod(g, 2)
                    g2 = 2 * TC * o + g
                    if o == 1 and g == 0:
                        pe.wait_ge(sem("gated"), 2 * KD)
                    if g2 >= 2:
                        pe.wait_ge(sem(f"ztok_set{g2 % 2}"), g2 // 2)
                    lo, hi = conv_cols(c * P, (c + 1) * P)
                    for k in range(4):
                        last = tr(bank[2 + g % 2][:, k * P:(k + 1) * P], st[:, 2, 4 * hf + k, lo:hi], ident)
                    last.then_inc(sem("ztok_mm"), 1)
                for v in range(2):
                    pe.wait_ge(sem(f"ztok_set{v}"), TC * (o + 1))
                if o == 0:
                    pe.wait_ge(sem("u_set"), 48)
                for i in range(6):
                    r, hf = divmod(i, 2)
                    g = 6 * o + i
                    if g >= 2:
                        pe.wait_ge(sem("zf_used"), g - 1)
                    for part in range(2):
                        b = bank[4 + 2 * (g % 2) + part]
                        if r < 2:
                            ops = [(C["fwd256"], c * 512 + part * 256 + r * P, 1 + c) for c in range(2)]
                        else:
                            ops = [(C["fwd128"], part * P, 0)]
                        for j, (m, off, c) in enumerate(ops):
                            last = mm(b[:, :], m[:, off:off + P], ztok[:, c, hf * HALF:(hf + 1) * HALF],
                                      start=(j == 0), stop=(j == len(ops) - 1))
                    last.then_inc(sem("zf_mm"), 1)
                pe.wait_ge(sem("cprod"), 6 * (o + 1))
                for k in range(KD):
                    g = KD * o + k
                    if g >= 2:
                        pe.wait_ge(sem("gated"), 2 * (g - 1))
                    ks = slice(k * P, (k + 1) * P)
                    for j in range(2):
                        mm(bank[g % 2][:, 0:P], Yf[:, 4 + j, ks], C["inv128"][:, j * P:(j + 1) * P],
                           start=(j == 0), stop=(j == 1))
                    for j in range(4):
                        last = mm(bank[g % 2][:, P:T], Yf[:, j, ks], C["inv256"][:, j * DEC:(j + 1) * DEC],
                                  start=(j == 0), stop=(j == 3))
                    last.then_inc(sem("inv_mm"), 1)
            pe.wait_ge(sem("wout_in"), 16)
            pe.wait_ge(sem("gated"), 4 * KD)
            for m in range(KD):
                if m >= 2:
                    pe.wait_ge(sem("mix1_done"), 2 * (m - 1))
                for lo, hi in SPANS:
                    a0, a1 = conv_cols(lo, hi)
                    for k in range(KD):
                        last = mm(bank[4 + m % 2][:, lo:hi], wout[:, k, m * P:(m + 1) * P], st[:, 2, k, a0:a1],
                                  start=(k == 0), stop=(k == KD - 1))
                last.then_inc(sem("mix1_mm"), 1)
                if m >= 2:
                    norm_sum(3, m - 2)
            for k in (KD - 2, KD - 1):
                norm_sum(3, k)
            pe.wait_ge(sem("mix1_done"), 2 * KD)
            moe(1, 3)

            pe.wait_ge(sem("h_done"), 2 * KD * 4 + KD)
            for g in range(2 * TC):
                c, hf = divmod(g, 2)
                if g >= 2:
                    pe.wait_ge(sem("yout_done"), g - 1)
                for k in range(4):
                    last = tr(bank[4 + g % 2][:, k * P:(k + 1) * P], hT[:, 4 * hf + k, c * P:(c + 1) * P], ident)
                last.then_inc(sem("yout_mm"), 1)

        def qk_root(act, fn, m):
            act.wait_ge(sem("qss_mm"), m + 1)
            if m >= 2:
                act.wait_ge(sem("qn_set"), m - 1)
            fn(rq[:, m % 2, :], bank[4 + m % 2][:, 0:T], ACT.Sqrt, scale=1.0 / HD, bias=eps_col[:, 0:1])\
                .then_inc(sem("qrt_set"), 1)

        @block.scalar
        def _(act):
            fn = nc.scalar.activation

            act.wait_ge(sem("preset"), 3)
            act.wait_ge(sem("pc_done"), 1)
            fn(condS[:, :, 0], pc[:, R_CCTX:R_CCTX + KD], ACT.Silu).then_inc(sem("cond_set"), 1)
            fn(condS[:, :, 1], pc[:, R_C:R_C + KD], ACT.Silu).then_inc(sem("cond_set"), 1)
            for i in range(2):
                act.wait_ge(sem("angle_set"), i + 1)
                fn(hd1[0:FH, i, :], hdr[0:FH, i, :], ACT.Sin).then_inc(sem("mlp_done"), 1)

            def adaR_copy(t):
                act.wait_ge(sem("ada_mm"), t + 1)
                if t >= 2:
                    act.wait_ge(sem("ada_tr"), t - 1)
                fn(adaR[:, t % 2, :], bank[t % 2][:, 0:256], ACT.Copy).then_inc(sem("adaR_set"), 1)

            def taps(f):
                act.wait_ge(sem(f"decay_in{f % 2}"), 32 * (f // 2 + 1))
                for d in range(2):
                    fn(eld[:, f % 2, d, :], eld[:, f % 2, d, :], ACT.Exp).then_inc(sem("rate_set"), 1)
                act.wait_ge(sem("rate_set"), 2 * (f + 1))
                for i in range(7):
                    g = 6 * f + i
                    d, c = divmod(i, 3)
                    if i < 6:
                        if g >= 2:
                            act.wait_ge(sem("taps_done"), g - 1)
                        fn(dec[:, g % 2, :], eld[:, f % 2, d, :], ACT.Exp, scale=C["tneg"][:, c:c + 1])\
                            .then_inc(sem("dec_set"), 1)
                    if i >= 1:
                        g, (d, c) = g - 1, divmod(i - 1, 3)
                        act.wait_ge(sem("taps_done"), g + 1)
                        if g >= 2:
                            act.wait_ge(sem("size_mm"), g - 1)
                        fn(absb[:, g % 2, :], hfb[:, d, c, :], ACT.Abs).then_inc(sem("abs_done"), 1)

            def spectra(f):
                for i in range(6):
                    g = 6 * f + i
                    act.wait_ge(sem("cf_set"), g + 1)
                    o, n = FILT[f]
                    act.dma_start(cfD[o][:, i, n * HALF:(n + 1) * HALF], cfb[:, i, :]).then_inc(sem("cf_out"), 16)

            for t in range(NADA):
                adaR_copy(t)
                if t in FILT_AFTER:
                    taps(FILT_AFTER[t])
                if t - 1 in FILT_AFTER:
                    spectra(FILT_AFTER[t - 1])

            def squares(n, x_set, base=0, step=2):
                for k in range(KD):
                    g = KD * n + k
                    act.wait_ge(sem(x_set), base + step * (k + 1))
                    if g >= 2:
                        act.wait_ge(sem("sq_mm"), g - 1)
                    fn(sq[:, k % 2, :], xT[:, k, :], ACT.Square).then_inc(sem("sq_done"), 1)
                act.wait_ge(sem("sq_mm"), KD * (n + 1))
                fn(rstd[:, :], bank[3][:, 0:T], ACT.Sqrt, scale=1.0 / D, bias=eps_col[:, 0:1]).then_inc(sem("rt_done"), 1)

            def modulate(n, l, which):
                for k in range(KD):
                    act.wait_ge(sem("xn_set"), KD * n + k + 1)
                    for c, (lo, hi) in enumerate(SPANS):
                        fn(hT[:, k, lo:hi], hT[:, k, lo:hi], ACT.Identity, scale=amul[:, l, which, k, c:c + 1],
                           bias=ada[:, l, 3 * which, k, c:c + 1]).then_inc(sem("h_done"), 1)

            act.wait_ge(sem("ada_tr"), NADA)
            squares(0, "xT_done", step=1)
            modulate(0, 0, 0)
            for m in range(QK):
                act.wait_ge(sem("qk_mm"), m + 1)
                if m >= 2:
                    act.wait_ge(sem("qss_mm"), m - 1)
                fn(sq[:, m % 2, :], bank[m % 2][:, 0:T], ACT.Square).then_inc(sem("qsq_set"), 1)
                if m >= 1:
                    qk_root(act, fn, m - 1)
            qk_root(act, fn, QK - 1)
            for c in range(TC):
                act.wait_ge(sem("v_mm"), c + 1)
                fn(V[:, c, :], bank[c % 2][:, 0:256], ACT.Copy).then_inc(sem("v_done"), 1)
            act.wait_ge(sem("ktok_mm"), 1)
            fn(ktok, bank[7][:, 0:256], ACT.Copy).then_inc(sem("ktok_done"), 1)

            def exps(n):
                act.wait_ge(sem("nb_set"), n + 1)
                if n >= 4:
                    act.wait_ge(sem("probT_mm"), n - 3)
                X, Z = bank[2 * (n % 2)], bank[2 * (n % 2) + 1]
                for i, src in enumerate((X[:, 0:T], Z[:, 0:T], Z[:, T:512])):
                    dst = prob[:, n % 4, i * T:i * T + (T if i < 2 else P)]
                    fn(dst, src, ACT.Exp, scale=HD ** -0.5, bias=nb[:, n % 2, i:i + 1],
                       accum_out=rsum[:, n % 2, i:i + 1]).then_inc(sem("exp_done"), 1)

            def probT_copy(j):
                act.wait_ge(sem("probT_mm"), j + 1)
                if j >= 4:
                    act.wait_ge(sem("oT_mm"), j - 3)
                fn(probT[:, j % 4, 0:512], bank[4][:, :], ACT.Copy).then_inc(sem("probTa_set"), 1)

            act.wait_ge(sem("kv_out"), 32)
            for n in range(NH + 2):
                if n < NH:
                    exps(n)
                if n >= 2:
                    probT_copy(n - 2)

            def moe(l, n_norm):
                S_, B_ = sem, lambda name: l * PER_LAYER[name]
                squares(n_norm, f"mix{l}_done")
                modulate(n_norm, l, 1)
                for g in range(2 * TC):
                    c, hf = divmod(g, 2)
                    act.wait_ge(S_("htok_mm"), B_("htok_mm") + g + 1)
                    dst = hTok[:, c, :].rearrange("p (k a) -> p a k", k=8)[:, 64 * hf:64 * (hf + 1), :]
                    fn(dst, bank[4 + g % 2].rearrange("p (a k) -> p a k", k=8), ACT.Copy).then_inc(S_("htok_set"), 1)
                act.wait_ge(S_("gsub_set"), B_("gsub_set") + 1)
                fn(gx.rearrange("p a b -> p (a b)"), gx.rearrange("p a b -> p (a b)"), ACT.Exp).then_inc(S_("gexp"), 1)
                act.wait_ge(S_("dv_set"), B_("dv_set") + 1)
                fn(ev.rearrange("p a b -> p (a b)"), ev.rearrange("p a b -> p (a b)"), ACT.Exp).then_inc(S_("gexp"), 1)
                for g in range(0, 2 * KD, 2):
                    act.wait_ge(S_("sort_mm"), B_("sort_mm") + g + 1)
                    fn(hS[:, g // 2, 0:T], bank[4 + g % 4][:, 0:T], ACT.Copy).then_inc(S_("sorted_act"), 1)

                def window_copy(dst, at, done):
                    off = act.value_load(woff[0:1, bass.ds(at, 1)], min_val=0, max_val=2 * T)
                    fn(dst[:, :, 0:WIN], hS[:, :, bass.ds(off, WIN)], ACT.Copy).then_inc(done, 1)

                def extra(q):
                    lo = act.value_load(cumx[0:1, bass.ds(q, 1)], min_val=0, max_val=2 * PAIRS)
                    hi = act.value_load(cumx[0:1, bass.ds(q + 1, 1)], min_val=0, max_val=2 * PAIRS)
                    with act.If(hi > lo):
                        with act.Fori(lo, hi) as x:
                            window_copy(GTx, further((x - lo + 1) * NE + 2 * q, NWIN * NE - 1), S_("xgt_set"))
                            act.wait_ge(S_("xgu_mm"), x + 1)
                            fn(S, bank[2][:, 0:EH], ACT.Silu).then_inc(S_("xsilu"), 1)
                            act.wait_ge(S_("xdn_mm"), x + 1)
                            act.wait_ge(S_("xy_free"), x + 1)
                            fn(Yx[:, 0:HALF], bank[4][:, :], ACT.Copy).then_inc(S_("xy_set"), 1)

                def pair(q, s, final):
                    extra(q)
                    act.wait_ge(S_("gu_mm"), B_("gu_mm") + q + 1)
                    fn(S, bank[2][:, 0:EH], ACT.Silu).then_inc(S_("silu"), 1)
                    if not final:
                        window_copy(GT, 2 * (q + 1), S_("gt_set"))
                    act.wait_ge(S_("dn_mm"), B_("dn_mm") + q + 2)
                    act.wait_ge(S_("y_free"), B_("y_free") + q + 1)
                    fn(Y[:, s, 0:HALF], bank[4 + 2 * s][:, :], ACT.Copy).then_inc(S_("y_set"), 1)

                act.wait_ge(S_("cum_set"), B_("cum_set") + 1)
                act.wait_ge(S_("sort_mm"), B_("sort_mm") + 2 * KD)
                act.wait_ge(S_("sorted_act"), B_("sorted_act") + KD)
                act.wait_ge(S_("sorted_dve"), B_("sorted_dve") + KD + 1)
                nc.scalar.nop().then_inc(S_("y_set"), 2)
                window_copy(GT, 0, S_("gt_set"))
                with act.Fori(0, PAIRS // 2 - 1) as i:
                    for s in range(2):
                        pair(2 * i + s, s, False)
                for s in range(2):
                    pair(PAIRS - 2 + s, s, s == 1)

            moe(0, 1)
            squares(2, "moe_add")
            modulate(2, 1, 0)
            for n in range(24):
                stream, k = divmod(WIN_ORDER[n // 4] * 4 + n % 4, KD)
                act.wait_ge(sem("hin_mm"), n + 1)
                if n >= 2:
                    act.wait_ge(sem("conv_done"), n - 1)
                else:
                    act.wait_ge(sem("upad_clear"), 1)
                r = R_BIN + stream * KD + k
                for lo, hi in SPANS:
                    a0, a1 = conv_cols(lo, hi)
                    fn(upad[:, n % 2, a0 + 1:a1 + 1], bank[n % 2][:, lo:hi], ACT.Identity, bias=pc[:, r:r + 1])\
                        .then_inc(sem("u_set"), 1)
            for o in range(2):
                for g in range(0, 2 * TC, 2):
                    c, hf = divmod(g, 2)
                    act.wait_ge(sem("ztok_mm"), 2 * TC * o + g + 1)
                    if g == 0:
                        act.wait_ge(sem("hin_mm"), 24)
                    fn(ztok[:, c, 0:HALF], bank[2][:, :], ACT.Copy).then_inc(sem("ztok_set0"), 1)
            moe(1, 3)
            squares(4, "moe_add", PER_LAYER["moe_add"])
            for k in range(KD):
                act.wait_ge(sem("xn_set"), KD * 4 + k + 1)
                fn(hT[:, k, :], hT[:, k, :], ACT.Copy, scale=pc[:, R_FIN + k:R_FIN + k + 1]).then_inc(sem("h_done"), 1)

        @block.vector
        def _(dve):
            v = nc.vector
            chain = [0]

            def link(ins):
                chain[0] += 1
                ins.then_inc(sem("dve_chain"), 1)
                dve.wait_ge(sem("dve_chain"), chain[0])

            v.memset(none_tile, NONE).then_inc(sem("preset"), 1)
            v.memset(condS[:, :, :], 0.0).then_inc(sem("preset"), 1)
            v.memset(eps_col[:, :], EPS).then_inc(sem("preset"), 1)
            dve.wait_ge(sem("pc_mm"), 1)
            v.tensor_copy(pc[:, :], bank[7][:, 0:R_END]).then_inc(sem("pc_done"), 1)
            for k in range(KD):
                dve.wait_ge(sem("xT_mm"), k + 1)
                v.tensor_copy(xT[:, k, :], bank[k % 4][:, 0:T]).then_inc(sem("xT_done"), 1)
            dve.wait_ge(sem("xT_done"), KD)

            TURN = 2 * np.pi
            HI = float(np.float32(6.28125))
            LO = float(np.float32(TURN - 6.28125))
            BIG = float(1.5 * 2 ** 23)
            for i in range(2):
                dve.wait_ge(sem("mlp_mm"), i + 1)
                x, t = hdr[0:FH, i, :], hdt[0:FH, :]
                link(v.tensor_scalar(x, bank[4 + i][0:FH, 0:T], fcol[:, i:i + 1], fcol[:, 2:3], ALU.add, ALU.mult))
                link(v.tensor_scalar(t, x, float(1 / TURN), BIG, ALU.mult, ALU.add))
                link(v.tensor_scalar(t, t, BIG, None, ALU.subtract))
                link(v.scalar_tensor_tensor(x, t, -HI, x, ALU.mult, ALU.add))
                link(v.scalar_tensor_tensor(x, t, -LO, x, ALU.mult, ALU.add))
                if i == 1:
                    link(v.memset(hd1[FH:FH + 1, 1, :], 1.0))
                v.tensor_scalar(x, x, PI_F, -PI_F, ALU.min, ALU.max).then_inc(sem("angle_set"), 1)

            def ada_add(t):
                l, s = divmod(t, 6)
                dve.wait_ge(sem("ada_tr"), t + 1)
                for u in range(2):
                    src = bank[2][:, u * P:(u + 1) * P].rearrange("p (j c) -> p j c", j=4)[:, :, 0:2]
                    dst = ada[:, l, s].rearrange("p (j u) c -> p u j c", u=2)[:, u]
                    r = R_BADA + l * 48 + s * KD
                    bia = pc[:, r:r + KD].rearrange("p (j u a) -> p u j a", u=2, a=1)[:, u].to_broadcast([P, 4, 2])
                    last = v.tensor_tensor(dst, src, bia, ALU.add)
                last.then_inc(sem("ada_done"), 1)

            def taps(f):
                for i in range(6):
                    g = 6 * f + i
                    d, c = divmod(i, 3)
                    dve.wait_ge(sem("taps_mm"), g + 1)
                    dve.wait_ge(sem("dec_set"), g + 1)
                    if i == 0 and f > 0:
                        dve.wait_ge(sem("abs_done"), 6 * f)
                        dve.wait_ge(sem("smdf_done"), 6 * f)
                        dve.wait_ge(sem("cf_mm"), 6 * f)
                    v.tensor_tensor(hfb[:, d, c, :], bank[4 + g % 2][:, :], dec[:, g % 2, :], ALU.mult)\
                        .then_inc(sem("taps_done"), 1)
                dve.wait_ge(sem("taps_done"), 6 * (f + 1))
                if f > 0:
                    dve.wait_ge(sem("cf_mm"), 6 * f)
                    dve.wait_ge(sem("cf_set"), 6 * f)
                for d in range(2):
                    for c in range(3):
                        v.tensor_tensor(smdf[:, d, c, :], hfb[:, 0, c, :], hfb[:, 1, c, :], ALU.subtract if d else ALU.add)\
                            .then_inc(sem("smdf_done"), 1)
                dve.wait_ge(sem("size_mm"), 6 * (f + 1))
                for b in range(2):
                    link(v.tensor_scalar(rn[:, b, :], bank[6 + b][:, :], EPS, None, ALU.add))
                    v.reciprocal(rn[:, b, :], rn[:, b, :]).then_inc(sem("rn_set"), 1)

            def spectra(f):
                dve.wait_ge(sem("rn_set"), 2 * (f + 1))
                for i in range(6):
                    g = 6 * f + i
                    dve.wait_ge(sem("cf_mm"), g + 1)
                    if f > 0:
                        dve.wait_ge(sem("cf_out"), 16 * 6 * f)
                    v.tensor_tensor(cfb[:, i, :], bank[4 + g % 2][:, :], rn[:, 0 if i >= 4 else 1, :], ALU.mult)\
                        .then_inc(sem("cf_set"), 1)

            for t in range(NADA):
                if t >= 1:
                    ada_add(t - 1)
                if t in FILT_AFTER:
                    taps(FILT_AFTER[t])
                if t - 1 in FILT_AFTER:
                    spectra(FILT_AFTER[t - 1])
            ada_add(NADA - 1)
            dve.wait_ge(sem("ada_done"), NADA)
            for l in range(DEPTH):
                for w, r0 in ((0, R_NMIX), (1, R_NFFN)):
                    gain = pc[:, r0 + l * KD:r0 + (l + 1) * KD].rearrange("p (k a) -> p k a", a=1).to_broadcast([P, KD, 2])
                    link(v.scalar_tensor_tensor(amul[:, l, w], ada[:, l, 3 * w + 1], 1.0, gain, ALU.add, ALU.mult))
            bo = pc[:, R_BOUT:R_BOUT + KD].rearrange("p (k a) -> p k a", a=1).to_broadcast([P, KD, 2])
            link(v.tensor_tensor(gbo[:, :, :], ada[:, 1, 2], bo, ALU.mult))

            def norm(n):
                dve.wait_ge(sem("rt_done"), n + 1)
                link(v.reciprocal(rstd[:, :], rstd[:, :]))
                for k in range(KD):
                    v.tensor_tensor(hT[:, k, :], xT[:, k, :], rstd[:, :], ALU.mult).then_inc(sem("xn_set"), 1)

            def add_mix(k, src, done, g, mmsem, base=0):
                dve.wait_ge(mmsem, base + k + 1)
                for c, (lo, hi) in enumerate(SPANS):
                    v.scalar_tensor_tensor(xT[:, k, lo:hi], src[:, lo:hi], g[:, k, c:c + 1], xT[:, k, lo:hi],
                                           ALU.mult, ALU.add).then_inc(done, 1)

            dve.wait_ge(sem("cf_out"), 16 * 24)
            norm(0)
            def qk_norm(m):
                dve.wait_ge(sem("qrt_set"), m + 1)
                link(v.reciprocal(rq[:, m % 2, :], rq[:, m % 2, :]))
                dve.wait_ge(sem("raw_set"), m + 1)
                v.tensor_tensor(chunk_dst(m, 0, T), raw[:, m % 2, :], rq[:, m % 2, :], ALU.mult).then_inc(sem("qn_set"), 1)

            dve.wait_ge(sem("cache_in"), 48)

            def qk_turn(m):
                dve.wait_ge(sem("rot_mm"), m + 1)
                if m >= 2:
                    dve.wait_ge(sem("qk_done"), m - 1)
                v.tensor_tensor(rs_[:, m % 2, :], bank[6 + m % 2][:, 0:DEC], C["sin"], ALU.mult).then_inc(sem("qs_set"), 1)
                x = chunk_dst(m, SEQ, T)
                link(v.tensor_tensor(x, x, C["cos"], ALU.mult))
                dve.wait_ge(sem("qs_set"), m + 1)
                v.tensor_tensor(x, x, rs_[:, m % 2, :], ALU.add).then_inc(sem("qk_done"), 1)

            for m in range(QK + 2):
                if m < QK:
                    dve.wait_ge(sem("qsq_set"), m + 1)
                    if m >= 2:
                        dve.wait_ge(sem("qn_set"), m - 1)
                    gain = pc[:, R_KN:R_KN + 1] if m < 2 else pc[:, R_QN:R_QN + 1]
                    v.tensor_scalar(raw[:, m % 2, :], bank[m % 2][:, 0:T], gain, None, ALU.mult).then_inc(sem("raw_set"), 1)
                if 1 <= m <= QK:
                    qk_norm(m - 1)
                if m >= 2:
                    qk_turn(m - 2)
            dve.wait_ge(sem("ck_mm"), 1)
            v.tensor_copy(kT[:, :, T:512], bank[6][:, 0:256].rearrange("p (c t) -> p c t", c=2)).then_inc(sem("ck_set"), 1)

            def maxima(n):
                dve.wait_ge(sem("score_mm"), n + 1)
                X, Z = bank[2 * (n % 2)], bank[2 * (n % 2) + 1]
                for i, src in enumerate((X[:, 0:T], Z[:, 0:T], Z[:, T:512])):
                    last = v.reduce_max(mx[:, n % 2, i:i + 1], src, axis=AX.X)
                link(last)
                v.tensor_scalar(nb[:, n % 2, :], mx[:, n % 2, :], -(HD ** -0.5), None, ALU.mult).then_inc(sem("nb_set"), 1)

            def probs(n):
                dve.wait_ge(sem("exp_done"), 3 * (n + 1))
                link(v.reciprocal(rinv[:, n % 2, :], rsum[:, n % 2, :]))
                for i in range(3):
                    x = prob[:, n % 4, i * T:i * T + (T if i < 2 else P)]
                    last = v.tensor_scalar(x, x, rinv[:, n % 2, i:i + 1], None, ALU.mult)
                    last.then_inc(sem("prob_done"), 1)

            def probT_copy(j):
                dve.wait_ge(sem("probT_mm"), j + 1)
                if j >= 4:
                    dve.wait_ge(sem("oT_mm"), j - 3)
                v.tensor_copy(probT[:, j % 4, 512:896], bank[5][:, 0:T]).then_inc(sem("probTb_set"), 1)

            dve.wait_ge(sem("kv_out"), 32)
            for c in range(KD + 2):
                if c < KD:
                    maxima(2 * c)
                if 1 <= c <= KD:
                    probT_copy(2 * c - 2)
                if c < KD:
                    maxima(2 * c + 1)
                if c >= 2:
                    dve.wait_ge(sem("oT_mm"), 2 * (c - 1))
                    v.tensor_copy(oT[:, c - 2, :], bank[6 + c % 2][:, 0:T]).then_inc(sem("oT_set"), 1)
                if 1 <= c <= KD:
                    probT_copy(2 * c - 1)
                if c < KD:
                    probs(2 * c)
                    probs(2 * c + 1)
            for k in range(KD):
                add_mix(k, bank[k % 2], sem("mix0_done"), ada[:, 0, 2], sem("mix0_mm"))
            dve.wait_ge(sem("mix0_done"), 2 * KD)

            def bc(x, *shape):
                return x.to_broadcast(list(shape))

            def router(l):
                S_, B_ = sem, lambda name: l * PER_LAYER[name]
                dve.wait_ge(S_("logit_mm"), B_("logit_mm") + 1)
                src = bank[0][:, 0:TC * 64].rearrange("p (c e) -> p c e", c=TC)[:, :, 0:NG + NE]
                bias = rbias[:, l:l + 1, :].to_broadcast([P, TC, NG + NE])
                v.tensor_tensor(lg, src, bias, ALU.add).then_inc(S_("lg_set"), 1)
                dve.wait_ge(S_("lg_set"), B_("lg_set") + 1)
                g_ = lg[:, :, 0:NG]
                pr_g = C["prio"][:, 0:NG].rearrange("p (a g) -> p a g", a=1).to_broadcast([P, TC, NG])
                pr_e = C["prio"][:, NG:NG + EG].rearrange("p (a g) -> p a g", a=1).to_broadcast([P, TC, EG])
                link(v.reduce_max(gmax, g_, axis=AX.X))
                v.tensor_tensor(gx, g_, bc(gmax, P, TC, NG), ALU.subtract).then_inc(S_("gsub_set"), 1)
                first(g_, gmax, geq, v2, goh, pr_g, NG)
                go = goh.rearrange("p c (g a) -> p c g a", a=1).to_broadcast([P, TC, NG, EG])
                pick = mtmp[0][:, 0].rearrange("p c (g e) -> p c g e", g=NG)
                link(v.tensor_tensor(pick, lg[:, :, NG:].rearrange("p c (g e) -> p c g e", g=NG), go, ALU.mult))
                link(v.reduce_sum(esel, pick.rearrange("p c g e -> p c e g"), axis=AX.X))
                link(v.reduce_max(v1, esel, axis=AX.X))
                first(esel, v1, eeq, den, oh1, pr_e, EG)
                link(v.tensor_scalar(e2, oh1, -1.0, 1.0, ALU.mult, ALU.add))
                link(v.tensor_tensor(e2, esel, e2, ALU.mult))
                link(v.scalar_tensor_tensor(e2, oh1, -3.0e38, e2, ALU.mult, ALU.add))
                link(v.reduce_max(v2, e2, axis=AX.X))
                first(e2, v2, eeq, den, oh2, pr_e, EG)
                for k, oh in enumerate((oh1, oh2)):
                    m_ = masks[:, k].rearrange("p c (g e) -> p c g e", g=NG)
                    eo = oh.rearrange("p c (a e) -> p c a e", a=1).to_broadcast([P, TC, NG, EG])
                    last = v.tensor_tensor(m_, go, eo, ALU.mult)
                link(last)
                v.tensor_tensor(m_all, masks[:, 0], masks[:, 1], ALU.add).then_inc(S_("mask_set"), 1)
                v.tensor_tensor(ev, v2, v1, ALU.subtract).then_inc(S_("dv_set"), 1)
                def place_of(src):
                    return src.rearrange("p (a e) -> p a e", a=1)
                a_, b_ = start[:, 0], start[:, 1]
                link(v.memset(start, 0.0))
                dve.wait_ge(S_("place_mm"), B_("place_mm") + 1)
                link(v.tensor_copy(a_[:, 1:1 + NE], bank[1][:, 256:256 + NE]))
                for sh in (1, 2, 4, 8, 16):
                    v.tensor_copy(b_[:, 0:sh], a_[:, 0:sh])
                    link(v.tensor_tensor(b_[:, sh:NE + 1], a_[:, sh:NE + 1], a_[:, 0:NE + 1 - sh], ALU.add))
                    a_, b_ = b_, a_
                place = bank[1][:, 0:TC * 64].rearrange("p (c e) -> p c e", c=TC)[:, :, 0:NE]
                for i, (src, dst) in enumerate(((place, posk), (place_of(a_[:, 0:NE]), startk), (place_of(C["rowbase"]), basek))):
                    for k in range(2):
                        last = v.tensor_tensor(mtmp[i][:, k], src.to_broadcast([P, TC, NE]) if i else src, masks[:, k], ALU.mult)
                    link(last)
                    last = v.reduce_sum(dst, mtmp[i], axis=AX.X)
                link(last)
                link(v.tensor_tensor(spos, posk, startk, ALU.add))
                dve.wait_ge(S_("iota_in"), B_("iota_in") + 16)
                for c in range(TC):
                    last = v.tensor_scalar(onehot[:, c, :], iota, spos[:, 0, c:c + 1], None, ALU.is_equal)
                link(last)
                for c in range(TC):
                    v.scalar_tensor_tensor(onehot[:, c, :], iota, spos[:, 1, c:c + 1], onehot[:, c, :], ALU.is_equal, ALU.add)\
                        .then_inc(S_("onehot"), 1)
                dve.wait_ge(S_("gexp"), B_("gexp") + 2)
                link(v.reduce_sum(gden, gx, axis=AX.X))
                link(v.tensor_scalar(den, ev, 1.0, None, ALU.add))
                link(v.tensor_tensor(den, den, gden, ALU.mult))
                link(v.reciprocal(wck[:, 0], den[:, :, 0]))
                link(v.tensor_tensor(wck[:, 1], wck[:, 0], ev[:, :, 0], ALU.mult))
                link(v.tensor_scalar(wink, posk, -(WIN - 1) / 2, 1.0 / WIN, ALU.add, ALU.mult))
                link(v.tensor_scalar(wink, wink, BIG, None, ALU.add))
                link(v.tensor_scalar(wink, wink, BIG, float((P - WIN) * PAIRS), ALU.subtract, ALU.mult))
                link(v.scalar_tensor_tensor(rowk, posk, float(PAIRS), basek, ALU.mult, ALU.add))
                link(v.tensor_tensor(rowk, rowk, wink, ALU.add))
                link(v.tensor_copy(idx[:, :], rowk.rearrange("p a b -> p (a b)")))
                link(v.tensor_copy(pay[:, :, :, :].rearrange("p a b c -> p (a b c)"), trow[:, :]))
                v.tensor_copy(pay[:, :, :, 2].bitcast(F32), wck).then_inc(S_("slots_set"), 1)
                c1, c2 = cnt[:, 0:PAIRS + 1], cnt[:, 32:32 + PAIRS + 1]
                wo_ = cnt[:, 128:128 + NWIN * NE]
                for w in range(NWIN):
                    last = v.tensor_scalar(wo_[:, w * NE:(w + 1) * NE], a_[0:1, 0:NE], float(w * WIN), float(2 * T), ALU.add, ALU.min)
                link(last)
                link(v.tensor_copy(woff[:, :], wo_))
                link(v.memset(c1, 0.0))
                if l > 0:
                    link(v.tensor_copy(c1[:, 0:1], cumx[:, PAIRS:PAIRS + 1]))
                big = cnt[:, 96:96 + PAIRS]
                link(v.tensor_copy(cnt[:, 64:64 + NE], bank[1][0:1, 256:256 + NE]))
                pr = cnt[:, 64:64 + NE].rearrange("p (q j) -> p q j", j=2)
                link(v.tensor_tensor(big, pr[:, :, 0], pr[:, :, 1], ALU.max))
                link(v.tensor_scalar(big, big, -(WIN + 1) / 2, 1.0 / WIN, ALU.add, ALU.mult))
                link(v.tensor_scalar(big, big, BIG, None, ALU.add))
                link(v.tensor_scalar(c1[:, 1:PAIRS + 1], big, BIG, 0.0, ALU.subtract, ALU.max))
                src_, dst_ = c1, c2
                for sh in (1, 2, 4, 8):
                    link(v.tensor_copy(dst_[:, 0:sh], src_[:, 0:sh]))
                    link(v.tensor_tensor(dst_[:, sh:PAIRS + 1], src_[:, sh:PAIRS + 1], src_[:, 0:PAIRS + 1 - sh], ALU.add))
                    src_, dst_ = dst_, src_
                v.tensor_copy(cumx[:, :], src_).then_inc(S_("cum_set"), 1)

            def first(x, top, eq, key, oh, prio, n):
                link(v.tensor_tensor(eq, x, bc(top, P, TC, n), ALU.is_equal))
                link(v.tensor_tensor(eq, eq, prio, ALU.mult))
                link(v.reduce_max(key, eq, axis=AX.X))
                link(v.tensor_tensor(oh, eq, bc(key, P, TC, n), ALU.is_equal))

            def moe(l, n_norm):
                S_, B_ = sem, lambda name: l * PER_LAYER[name]
                norm(n_norm)
                router_and_rows(l)

                def window_copy(dst, at, done):
                    off = dve.value_load(woff[0:1, bass.ds(at, 1)], min_val=0, max_val=2 * T)
                    v.tensor_copy(dst[:, :, WIN:P], hS[:, :, bass.ds(off, WIN)]).then_inc(done, 1)

                def extra(q):
                    lo = dve.value_load(cumx[0:1, bass.ds(q, 1)], min_val=0, max_val=2 * PAIRS)
                    hi = dve.value_load(cumx[0:1, bass.ds(q + 1, 1)], min_val=0, max_val=2 * PAIRS)
                    with dve.If(hi > lo):
                        with dve.Fori(lo, hi) as x:
                            window_copy(GTx, further((x - lo + 1) * NE + 2 * q + 1, NWIN * NE - 1), S_("xgt_set"))
                            dve.wait_ge(S_("xslots"), x + 1)
                            dve.wait_ge(S_("xsilu"), x + 1)
                            v.scalar_tensor_tensor(A, bank[2][:, EH:2 * EH], curx[:, 2:3].bitcast(F32), S, ALU.mult, ALU.mult)\
                                .then_inc(S_("xact_set"), 1)
                            dve.wait_ge(S_("xat_mm"), x + 1)
                            v.tensor_copy(AT, bank[3][:, 0:256].rearrange("p (k s) -> p k s", k=2)).then_inc(S_("xat_set"), 1)
                            dve.wait_ge(S_("xdn_mm"), x + 1)
                            dve.wait_ge(S_("xy_free"), x + 1)
                            v.tensor_copy(Yx[:, HALF:D], bank[5][:, :]).then_inc(S_("xy_set"), 1)

                def pair(q, s, final):
                    extra(q)
                    dve.wait_ge(S_("slots"), B_("slots") + q + 1)
                    dve.wait_ge(S_("silu"), B_("silu") + q + 1)
                    v.scalar_tensor_tensor(A, bank[2][:, EH:2 * EH], cur[:, s, 2:3].bitcast(F32), S, ALU.mult, ALU.mult)\
                        .then_inc(S_("act_set"), 1)
                    if not final:
                        window_copy(GT, 2 * (q + 1) + 1, S_("gt_set"))
                    dve.wait_ge(S_("at_mm"), B_("at_mm") + q + 1)
                    v.tensor_copy(AT, bank[3][:, 0:256].rearrange("p (k s) -> p k s", k=2)).then_inc(S_("at_set"), 1)
                    dve.wait_ge(S_("dn_mm"), B_("dn_mm") + q + 2)
                    dve.wait_ge(S_("y_free"), B_("y_free") + q + 1)
                    v.tensor_copy(Y[:, s, HALF:D], bank[5 + 2 * s][:, :]).then_inc(S_("y_set"), 1)

                for g in range(1, 2 * KD, 2):
                    dve.wait_ge(S_("sort_mm"), B_("sort_mm") + g + 1)
                    v.tensor_copy(hS[:, g // 2, T:2 * T], bank[4 + g % 4][:, 0:T]).then_inc(S_("sorted_dve"), 1)
                dve.wait_ge(S_("sorted_act"), B_("sorted_act") + KD)
                dve.wait_ge(S_("sorted_dve"), B_("sorted_dve") + KD + 1)
                dve.wait_ge(S_("cum_set"), B_("cum_set") + 1)
                nc.vector.nop().then_inc(S_("act_set"), 1)
                nc.vector.nop().then_inc(S_("y_set"), 2)
                window_copy(GT, 1, S_("gt_set"))
                with dve.Fori(0, PAIRS // 2 - 1) as i:
                    for s in range(2):
                        pair(2 * i + s, s, False)
                for s in range(2):
                    pair(PAIRS - 2 + s, s, s == 1)
                for k in range(KD):
                    if k % (KD // 2) == 0:
                        hf = k // (KD // 2)
                        dve.wait_ge(S_(f"y2_in{hf}_"), B_(f"y2_in{hf}_") + 32)
                    ks = slice(k * P, (k + 1) * P)
                    v.tensor_tensor(y2[:, 0, :, ks], y2[:, 0, :, ks], y2[:, 1, :, ks], ALU.add).then_inc(S_("ysum"), 1)
                    if k >= 1:
                        add_mix(k - 1, bank[(k - 1) % 2], S_("moe_add"), ada[:, l, 5], S_("res_mm"), B_("res_mm"))
                add_mix(KD - 1, bank[(KD - 1) % 2], S_("moe_add"), ada[:, l, 5], S_("res_mm"), B_("res_mm"))
                dve.wait_ge(S_("moe_add"), B_("moe_add") + 2 * KD)

            def router_and_rows(l):
                S_, B_ = sem, lambda name: l * PER_LAYER[name]
                if l == 0:
                    dve.wait_ge(sem("kv_out"), 32)
                v.memset(hS[:, :, 2 * T:], 0.0).then_inc(S_("sorted_dve"), 1)
                router(l)

            moe(0, 1)
            norm(2)
            v.memset(upad[:, :, :], 0.0).then_inc(sem("upad_clear"), 1)
            for n in range(24):
                stream, k = divmod(WIN_ORDER[n // 4] * 4 + n % 4, KD)
                dve.wait_ge(sem("u_set"), 2 * (n + 1))
                if n >= 2:
                    dve.wait_ge(sem("conv_done"), n - 1)
                u, t = upad[:, n % 2, :], cv[:, n % 2, :]
                w = lambda i: pc[:, R_SW + i * 24 + stream * KD + k:R_SW + i * 24 + stream * KD + k + 1]
                r = R_SB + stream * KD + k
                link(v.tensor_scalar(t, u[:, 0:UW], w(0), pc[:, r:r + 1], ALU.mult, ALU.add))
                link(v.scalar_tensor_tensor(t, u[:, 1:UW + 1], w(1), t, ALU.mult, ALU.add))
                v.scalar_tensor_tensor(st[:, stream, k, :], u[:, 2:UW + 2], w(2), t, ALU.mult, ALU.add)\
                    .then_inc(sem("conv_done"), 1)
            for o in range(2):
                for g in range(1, 2 * TC, 2):
                    c, hf = divmod(g, 2)
                    dve.wait_ge(sem("ztok_mm"), 2 * TC * o + g + 1)
                    v.tensor_copy(ztok[:, c, HALF:D], bank[3][:, :]).then_inc(sem("ztok_set1"), 1)
                dve.wait_ge(sem(f"cf_in{o}"), 16)
                for i in range(6):
                    r, hf = divmod(i, 2)
                    g = 6 * o + i
                    hs = slice(hf * HALF, (hf + 1) * HALF)
                    re, im = (r, 2 + r) if r < 2 else (4, 5)
                    dve.wait_ge(sem("zf_mm"), g + 1)
                    if o == 1 and i == 0:
                        dve.wait_ge(sem("inv_mm"), KD)
                    zr, zi = bank[4 + 2 * (g % 2)][:, :], bank[5 + 2 * (g % 2)][:, :]
                    rr, ii, ri, ir = [prod[:, j, :] for j in range(4)]
                    link(v.tensor_tensor(rr, zr, cf[:, re, hs], ALU.mult))
                    link(v.tensor_tensor(ii, zi, cf[:, im, hs], ALU.mult))
                    link(v.tensor_tensor(ri, zr, cf[:, im, hs], ALU.mult))
                    link(v.tensor_tensor(ir, zi, cf[:, re, hs], ALU.mult))
                    nc.vector.nop().then_inc(sem("zf_used"), 1)
                    link(v.tensor_tensor(Yf[:, im, hs], ri, ir, ALU.add))
                    if r != 1:
                        link(v.tensor_copy(Yf[0:1, im, hs], ii[0:1, :]))
                        link(v.memset(ii[0:1, :], 0.0))
                    link(v.tensor_tensor(Yf[:, re, hs], rr, ii, ALU.subtract))
                    nc.vector.nop().then_inc(sem("cprod"), 1)
                for k in range(KD):
                    g = KD * o + k
                    dve.wait_ge(sem("inv_mm"), g + 1)
                    sk = pc[:, R_SKIP + o * KD + k:R_SKIP + o * KD + k + 1]
                    if g >= 1:
                        dve.wait_ge(sem("gated"), 2 * g)
                    for lo, hi in SPANS:
                        a0, a1 = conv_cols(lo, hi)
                        link(v.scalar_tensor_tensor(ztmp[:, lo:hi], st[:, 2, k, a0:a1], sk, bank[g % 2][:, lo:hi],
                                                    ALU.mult, ALU.add))
                        v.tensor_tensor(st[:, 2, k, a0:a1], ztmp[:, lo:hi], st[:, o, k, a0:a1], ALU.mult)\
                            .then_inc(sem("gated"), 1)
                dve.wait_ge(sem("gated"), 2 * KD * (o + 1))
            for k in range(KD):
                dve.wait_ge(sem("mix1_mm"), k + 1)
                if k >= 1:
                    dve.wait_ge(sem("mix1_done"), 2 * k)
                for c, (lo, hi) in enumerate(SPANS):
                    link(v.tensor_scalar(ytmp[:, lo:hi], bank[4 + k % 2][:, lo:hi], ada[:, 1, 2, k, c:c + 1], gbo[:, k, c:c + 1],
                                         ALU.mult, ALU.add))
                    v.tensor_tensor(xT[:, k, lo:hi], xT[:, k, lo:hi], ytmp[:, lo:hi], ALU.add).then_inc(sem("mix1_done"), 1)
            dve.wait_ge(sem("mix1_done"), 2 * KD)
            moe(1, 3)
            norm(4)
            for g in range(2 * TC):
                c, hf = divmod(g, 2)
                dve.wait_ge(sem("yout_mm"), g + 1)
                v.tensor_copy(yout[:, c, hf * HALF:(hf + 1) * HALF], bank[4 + g % 2][:, :]).then_inc(sem("yout_done"), 1)

        @block.gpsimd
        def _(pool):
            ind = nc.gpsimd.indirect_dma_start

            def at_rows(ap):
                return bass.IndirectOffsetOnAxis(ap=ap.bitcast(U32), axis=0)

            def moe(l):
                S_, B_ = sem, lambda name: l * PER_LAYER[name]
                pool.wait_ge(S_("slots_set"), B_("slots_set") + 1)
                pool.wait_ge(sem("tab_clear"), 16 * DEPTH)
                for n in range(TC * 2):
                    ind(out=tabD[l], out_offset=at_rows(idx[:, n:n + 1]), in_=pay[:, n // TC, n % TC, :], in_offset=None,
                        bounds_check=NWIN * P * PAIRS - 1, oob_is_err=False).then_inc(S_("tab_fill"), 16)
                pool.wait_ge(S_("tab_fill"), B_("tab_fill") + 16 * TC * 2)
                pool.dma_start(tab.rearrange("p (w q) -> p w q", w=NWIN),
                               tabD[l].rearrange("(w p q) c -> p w (q c)", w=NWIN, p=P)).then_inc(S_("tab_in"), 16)
                pool.wait_ge(S_("tab_in"), B_("tab_in") + 16)
                pool.wait_ge(S_("cum_set"), B_("cum_set") + 1)

                def slots(dst, off, done):
                    nc.gpsimd.tensor_copy(dst, tab[:, bass.ds(off, 4)]).then_inc(done, 1)

                def scatter(src, ix, done):
                    apart(pool)
                    ind(out=yD, out_offset=at_rows(ix), in_=src, in_offset=None, bounds_check=2 * T - 1,
                        oob_is_err=False).then_inc(done, 16)

                def extra(q):
                    lo = pool.value_load(cumx[0:1, bass.ds(q, 1)], min_val=0, max_val=2 * PAIRS)
                    hi = pool.value_load(cumx[0:1, bass.ds(q + 1, 1)], min_val=0, max_val=2 * PAIRS)
                    with pool.If(hi > lo):
                        with pool.Fori(lo, hi) as x:
                            slots(curx[:, :], further(((x - lo + 1) * PAIRS + q) * 4, NWIN * PAIRS * 4 - 4), S_("xslots"))
                            nc.gpsimd.nop().then_inc(S_("xy_free"), 1)
                            pool.wait_ge(S_("xslots"), x + 1)
                            pool.wait_ge(S_("xy_set"), 2 * (x + 1))
                            scatter(Yx, curx[:, 0:1], S_("xscatter"))
                            pool.wait_ge(S_("xscatter"), 16 * (x + 1))

                def pair(q, s):
                    slots(cur[:, s, :], q * 4, S_("slots"))
                    extra(q)
                    pool.wait_ge(S_("slots"), B_("slots") + q + 1)
                    pool.wait_ge(S_("y_set"), B_("y_set") + 2 * q + 6)
                    scatter(Y[:, s, :], cur[:, s, 0:1], S_("scatter"))
                    pool.wait_ge(S_("scatter"), B_("scatter") + 16 * (q + 1))
                    nc.gpsimd.nop().then_inc(S_("y_free"), 1)

                nc.gpsimd.nop().then_inc(S_("y_free"), 2)
                with pool.Fori(0, PAIRS // 2) as i:
                    for s in range(2):
                        pair(2 * i + s, s)
                nc.gpsimd.nop().then_inc(S_("rows_done"), 1)

            moe(0)
            moe(1)


_INS = ['x_prompt', 'x_sample', 'cache_k', 'cache_v', 'c', 'c_ctx', 'w_ada', 'b_ada', 'norm_mix', 'norm_ffn',
        'attn_w_q', 'attn_w_kv', 'attn_q_norm', 'attn_k_norm', 'attn_w_o', 'hy_w_in', 'hy_b_in', 'hy_short_w',
        'hy_short_b', 'hy_filt_w1', 'hy_filt_b1', 'hy_filt_w2', 'hy_filt_b2', 'hy_filt_w3', 'hy_filt_b3',
        'hy_filt_freq', 'hy_log_decay', 'hy_skip', 'hy_w_out', 'hy_b_out', 'router_group_w', 'router_group_b',
        'router_expert_w', 'router_expert_b', 'moe_w_gate', 'moe_w_up', 'moe_w_down', 'final_norm']
_OUTS = [(1, SEQ, D), (1, DEC, D), (1, 1, NKV, SEQ, HD), (1, 1, NKV, SEQ, HD)]


def kernel(**inputs):
    import concourse.bacc as _bacc
    from concourse.bass_utils import run_bass_kernel_spmd as _run

    nc = _bacc.Bacc("TRN2", target_bir_lowering=False, num_devices=1)
    given = {n: np.ascontiguousarray(inputs[n]) for n in _INS}
    given["const"] = CONST
    given["token_rows"] = token_rows()
    arrays, args = {}, {}
    for name, x in given.items():
        arrays[f"in_{name}"] = x
        args[name] = nc.dram_tensor(f"in_{name}", x.shape, mybir.dt.from_np(x.dtype), kind="ExternalInput").ap()
    for i, shape in enumerate(_OUTS):
        args[f"out_{i}"] = nc.dram_tensor(f"out_{i}_dram", shape, F32, kind="ExternalOutput").ap()
    build(nc, args)
    r = _run(nc, [arrays], core_ids=[0])
    return tuple(r.results[0][f"out_{i}_dram"] for i in range(len(_OUTS)))
```
